# Optimizing a Trainium2 kernel written in Bass

```python
import jax, jax.numpy as jnp
from jax import lax
import numpy as np
import math

D_MODEL = 1024
BATCH = 1
SEQ = 256
DEPTH = 2

CHUNK = 64
EPS = 1e-6

HEAD_DIM = 64
ATTN_WIDTH = D_MODEL // 2
ATTN_HEADS = ATTN_WIDTH // HEAD_DIM
ROPE_DIM = HEAD_DIM // 4
ROPE_THETA = 500000.0
IDX_HEADS = 4
IDX_DIM = 64
IDX_SCALE = (IDX_DIM ** -0.5) * (IDX_HEADS ** -0.5)
TOPK_MAX = 256
QBLOCK = 64

CONV_WIDTH = D_MODEL // 2
CONV_GROUPS = 8
CONV_K = 3

N_BRANCH = 2
MLP_HIDDEN = 4 * D_MODEL

PROJ_SIZES = (ATTN_WIDTH, ATTN_WIDTH, ATTN_WIDTH, IDX_HEADS * IDX_DIM, IDX_DIM, IDX_HEADS,
              CONV_WIDTH, CONV_WIDTH, CONV_WIDTH, N_BRANCH * D_MODEL)
IN_COLS = sum(PROJ_SIZES)


def rmsnorm(x, g):
    xf = x.astype(jnp.float32)
    y = xf * lax.rsqrt(jnp.mean(xf * xf, axis=-1, keepdims=True) + EPS)
    return (y * g.astype(jnp.float32)).astype(x.dtype)

def rope_tables(T):
    inv = 1.0 / (ROPE_THETA ** (jnp.arange(0, ROPE_DIM, 2, dtype=jnp.float32) / ROPE_DIM))
    ang = jnp.arange(T, dtype=jnp.float32)[:, None] * inv[None, :]
    return jnp.cos(ang), jnp.sin(ang)

def apply_partial_rope(x, cos, sin):
    half = ROPE_DIM // 2
    xr = x[..., :ROPE_DIM].astype(jnp.float32)
    x1, x2 = xr[..., :half], xr[..., half:]
    c = cos[None, :, None, :]
    s = sin[None, :, None, :]
    rot = jnp.concatenate([x1 * c - x2 * s, x2 * c + x1 * s], axis=-1)
    return jnp.concatenate([rot.astype(x.dtype), x[..., ROPE_DIM:]], axis=-1)

def dsa_attention(q, k, v, iq, ik, iw):
    B, T, H, Dh = q.shape
    topk = min(TOPK_MAX, T // 4)
    nblk = T // QBLOCK
    key_pos = jnp.arange(T)
    scale = Dh ** -0.5
    ikf = ik.astype(jnp.float32)

    def block(i):
        t0 = i * QBLOCK
        qb = lax.dynamic_slice_in_dim(q, t0, QBLOCK, axis=1)
        iqb = lax.dynamic_slice_in_dim(iq, t0, QBLOCK, axis=1).astype(jnp.float32)
        iwb = lax.dynamic_slice_in_dim(iw, t0, QBLOCK, axis=1).astype(jnp.float32)
        tpos = t0 + jnp.arange(QBLOCK)
        limit = (tpos // CHUNK + 1) * CHUNK
        admissible = key_pos[None, :] < limit[:, None]
        logits = jnp.einsum('bthd,bsd->bths', iqb, ikf)
        score = jnp.einsum('bths,bth->bts', jax.nn.relu(logits), iwb) * IDX_SCALE
        score = jnp.where(admissible[None], score, -jnp.inf)
        _, idx = lax.top_k(score, topk)
        valid = idx < limit[None, :, None]
        kg = jax.vmap(lambda kk, ii: kk[ii])(k, idx)
        vg = jax.vmap(lambda vv, ii: vv[ii])(v, idx)
        s = jnp.einsum('bthd,btkhd->bthk', qb, kg).astype(jnp.float32) * scale
        s = jnp.where(valid[:, :, None, :], s, -jnp.inf)
        p = jax.nn.softmax(s, axis=-1).astype(v.dtype)
        return jnp.einsum('bthk,btkhd->bthd', p, vg)

    out = lax.map(block, jnp.arange(nblk))
    return out.transpose(1, 0, 2, 3, 4).reshape(B, T, H * Dh)

def short_conv(xc, conv_w):
    T = xc.shape[1]
    xp = jnp.pad(xc, ((0, 0), (CONV_K - 1, 0), (0, 0)))
    out = xp[:, 0:T] * conv_w[0]
    for j in range(1, CONV_K):
        out = out + xp[:, j:j + T] * conv_w[j]
    return out

def first_inputs(seed: int = 0) -> dict:
    key = jax.random.key(seed)
    ks = jax.random.split(key, 12)
    f32 = jnp.float32
    x = jax.random.normal(ks[0], (BATCH, SEQ, D_MODEL), f32)
    norm_mix = 1.0 + 0.02 * jax.random.normal(ks[1], (DEPTH, D_MODEL), f32)
    w_in = jax.random.normal(ks[2], (DEPTH, D_MODEL, IN_COLS), f32) * D_MODEL ** -0.5
    conv_w = jax.random.normal(ks[3], (DEPTH, CONV_K, CONV_WIDTH), f32) * CONV_K ** -0.5
    w_attn_out = jax.random.normal(ks[4], (DEPTH, ATTN_WIDTH, D_MODEL), f32) * ATTN_WIDTH ** -0.5
    w_conv_out = jax.random.normal(ks[5], (DEPTH, CONV_WIDTH, D_MODEL), f32) * CONV_WIDTH ** -0.5
    w_mix_out = jax.random.normal(ks[6], (DEPTH, D_MODEL, D_MODEL), f32) * D_MODEL ** -0.5
    norm_mlp = 1.0 + 0.02 * jax.random.normal(ks[7], (DEPTH, D_MODEL), f32)
    w_mlp_up = jax.random.normal(ks[8], (DEPTH, D_MODEL, MLP_HIDDEN), f32) * D_MODEL ** -0.5
    w_mlp_down = jax.random.normal(ks[9], (DEPTH, MLP_HIDDEN, D_MODEL), f32) * MLP_HIDDEN ** -0.5
    norm_final = 1.0 + 0.02 * jax.random.normal(ks[10], (D_MODEL,), f32)
    return {"x": x, "norm_mix": norm_mix, "w_in": w_in, "conv_w": conv_w,
            "w_attn_out": w_attn_out, "w_conv_out": w_conv_out, "w_mix_out": w_mix_out,
            "norm_mlp": norm_mlp, "w_mlp_up": w_mlp_up, "w_mlp_down": w_mlp_down,
            "norm_final": norm_final}

def first_block(x, norm_mix, w_in, conv_w, w_attn_out, w_conv_out, w_mix_out,
              norm_mlp, w_mlp_up, w_mlp_down, norm_final):
    B, T, D = x.shape
    cos, sin = rope_tables(T)
    offsets = np.cumsum(PROJ_SIZES)[:-1].tolist()
    for l in range(DEPTH):
        u = rmsnorm(x, norm_mix[l])
        proj = u @ w_in[l]
        q, k, v, iq, ik, iw, cB, cC, ch, g = jnp.split(proj, offsets, axis=-1)
        q = apply_partial_rope(q.reshape(B, T, ATTN_HEADS, HEAD_DIM), cos, sin)
        k = apply_partial_rope(k.reshape(B, T, ATTN_HEADS, HEAD_DIM), cos, sin)
        v = v.reshape(B, T, ATTN_HEADS, HEAD_DIM)
        iq = apply_partial_rope(iq.reshape(B, T, IDX_HEADS, IDX_DIM), cos, sin)
        ik = apply_partial_rope(ik[:, :, None, :], cos, sin)[:, :, 0, :]
        y_attn = dsa_attention(q, k, v, iq, ik, iw) @ w_attn_out[l]
        y_conv = (cB * short_conv(cC * ch, conv_w[l])) @ w_conv_out[l]
        gates = jax.nn.sigmoid(g.reshape(B, T, N_BRANCH, D))
        merged = gates[:, :, 0] * y_attn + gates[:, :, 1] * y_conv
        x = x + merged @ w_mix_out[l]
        u = rmsnorm(x, norm_mlp[l])
        x = x + jnp.square(jax.nn.relu(u @ w_mlp_up[l])) @ w_mlp_down[l]
    return rmsnorm(x, norm_final)


DEPTH_2 = 1

N_HEADS_A = 8
N_KV_A = 2
GROUP_A = N_HEADS_A // N_KV_A
N_HEADS_B = 8
WINDOW = 128
WIN_BLOCK = 128
T5_BUCKETS = 32
T5_MAX_DIST = 128
GRID_W = 64
NA_ROWS = 8
NA_COLS = 16
PEER_HEADS = 8
PEER_KEYS = 128
N_EXPERTS = PEER_KEYS * PEER_KEYS
PEER_QDIM = 256
PEER_HALF = PEER_QDIM // 2
PEER_TOPK = 16
PEER_CHUNK = 128
NEG = -1e30

W_QA = N_HEADS_A * HEAD_DIM
W_KVA = N_KV_A * HEAD_DIM
W_B = N_HEADS_B * HEAD_DIM
D_MIX = W_QA + W_B
D_IN = W_QA + 2 * W_KVA + 3 * W_B
IN_SPLITS = [W_QA, W_QA + W_KVA, W_QA + 2 * W_KVA, W_QA + 2 * W_KVA + W_B, W_QA + 2 * W_KVA + 2 * W_B]


def rms_norm(x, g):
    xf = x.astype(jnp.float32)
    y = xf * lax.rsqrt(jnp.mean(xf * xf, axis=-1, keepdims=True) + EPS)
    return (y * g.astype(jnp.float32)).astype(x.dtype)

def modulate(h, shift, scale):
    return h * (1.0 + scale[:, None, :]) + shift[:, None, :]

def t5_bucket(rel):
    half = T5_BUCKETS // 2
    max_exact = half // 2
    ret = jnp.where(rel > 0, half, 0)
    n = jnp.abs(rel)
    nf = jnp.maximum(n, 1).astype(jnp.float32)
    large = max_exact + (jnp.log(nf / max_exact) / math.log(T5_MAX_DIST / max_exact)
                         * (half - max_exact)).astype(jnp.int32)
    large = jnp.minimum(large, half - 1)
    return ret + jnp.where(n < max_exact, n, large)

def windowed_gqa(q, k, v, sink, t5_table):
    B, S = q.shape[0], q.shape[1]
    nb = S // WIN_BLOCK
    span = WIN_BLOCK + 2 * WINDOW
    pad = ((0, 0), (WINDOW, WINDOW), (0, 0), (0, 0))
    k_pad = jnp.pad(k, pad)
    v_pad = jnp.pad(v, pad)
    i = jnp.arange(WIN_BLOCK)[:, None]
    j = jnp.arange(span)[None, :]
    rel = j - WINDOW - i
    band = jnp.abs(rel) <= WINDOW
    bias = t5_table[t5_bucket(rel)].transpose(2, 0, 1).astype(jnp.float32)
    scale = HEAD_DIM ** -0.5
    sink_f = sink.astype(jnp.float32)

    def block(b):
        qb = lax.dynamic_slice_in_dim(q, b * WIN_BLOCK, WIN_BLOCK, axis=1)
        qb = qb.reshape(B, WIN_BLOCK, N_KV_A, GROUP_A, HEAD_DIM)
        kb = lax.dynamic_slice_in_dim(k_pad, b * WIN_BLOCK, span, axis=1)
        vb = lax.dynamic_slice_in_dim(v_pad, b * WIN_BLOCK, span, axis=1)
        s = jnp.einsum('bqgrd,bkgd->bgrqk', qb, kb).astype(jnp.float32)
        s = s.reshape(B, N_HEADS_A, WIN_BLOCK, span) * scale + bias
        kpos = b * WIN_BLOCK - WINDOW + jnp.arange(span)
        valid = band & ((kpos >= 0) & (kpos < S))[None, :]
        s = jnp.where(valid, s, NEG)
        sink_col = jnp.broadcast_to(sink_f[None, :, None, None], (B, N_HEADS_A, WIN_BLOCK, 1))
        p = jax.nn.softmax(jnp.concatenate([s, sink_col], axis=-1), axis=-1)[..., :span]
        p = p.astype(v.dtype).reshape(B, N_KV_A, GROUP_A, WIN_BLOCK, span)
        o = jnp.einsum('bgrqk,bkgd->bqgrd', p, vb)
        return o.reshape(B, WIN_BLOCK, N_HEADS_A * HEAD_DIM)

    out = lax.map(block, jnp.arange(nb))
    return out.transpose(1, 0, 2, 3).reshape(B, S, N_HEADS_A * HEAD_DIM)

def neighbourhood_attention(q, k, v, rpb):
    B, S = q.shape[0], q.shape[1]
    rows = S // GRID_W
    kr = min(NA_ROWS, rows)
    q_g = q.reshape(B, rows, GRID_W, N_HEADS_B, HEAD_DIM)
    k_g = k.reshape(B, rows, GRID_W, N_HEADS_B, HEAD_DIM)
    v_g = v.reshape(B, rows, GRID_W, N_HEADS_B, HEAD_DIM)
    cols = jnp.arange(GRID_W)
    col_start = jnp.clip(cols - NA_COLS // 2, 0, GRID_W - NA_COLS)
    col_idx = col_start[:, None] + jnp.arange(NA_COLS)[None, :]
    col_off = col_idx - cols[:, None] + (NA_COLS - 1)
    scale = HEAD_DIM ** -0.5
    rpb_f = rpb.astype(jnp.float32)

    def row_block(r):
        rs = jnp.clip(r - kr // 2, 0, rows - kr)
        q_r = lax.dynamic_index_in_dim(q_g, r, axis=1, keepdims=False)
        k_band = lax.dynamic_slice_in_dim(k_g, rs, kr, axis=1)
        v_band = lax.dynamic_slice_in_dim(v_g, rs, kr, axis=1)
        k_win = k_band[:, :, col_idx]
        v_win = v_band[:, :, col_idx]
        s = jnp.einsum('bchd,bkcwhd->bhckw', q_r, k_win).astype(jnp.float32) * scale
        row_off = rs + jnp.arange(kr) - r + (NA_ROWS - 1)
        bias = rpb_f[:, row_off[None, :, None], col_off[:, None, :]]
        s = (s + bias[None]).reshape(B, N_HEADS_B, GRID_W, kr * NA_COLS)
        p = jax.nn.softmax(s, axis=-1).reshape(B, N_HEADS_B, GRID_W, kr, NA_COLS).astype(v.dtype)
        return jnp.einsum('bhckw,bkcwhd->bchd', p, v_win)

    out = lax.map(row_block, jnp.arange(rows))
    return out.transpose(1, 0, 2, 3, 4).reshape(B, S, N_HEADS_B * HEAD_DIM)

def peer(h, w_query, sub_keys, u_experts, v_experts):
    B, S, D = h.shape
    tokens = h.reshape(B * S // PEER_CHUNK, PEER_CHUNK, D)

    def chunk(xc):
        qh = (xc @ w_query).reshape(PEER_CHUNK, PEER_HEADS, PEER_QDIM)
        s1 = jnp.einsum('thd,hnd->thn', qh[..., :PEER_HALF], sub_keys[:, 0]).astype(jnp.float32)
        s2 = jnp.einsum('thd,hnd->thn', qh[..., PEER_HALF:], sub_keys[:, 1]).astype(jnp.float32)
        v1, i1 = lax.top_k(s1, PEER_TOPK)
        v2, i2 = lax.top_k(s2, PEER_TOPK)
        cand = (v1[..., :, None] + v2[..., None, :]).reshape(PEER_CHUNK, PEER_HEADS, PEER_TOPK * PEER_TOPK)
        vs, ci = lax.top_k(cand, PEER_TOPK)
        e1 = jnp.take_along_axis(i1, ci // PEER_TOPK, axis=-1)
        e2 = jnp.take_along_axis(i2, ci % PEER_TOPK, axis=-1)
        idx = e1 * PEER_KEYS + e2
        g = jax.nn.softmax(vs, axis=-1)
        u_sel = u_experts[idx]
        v_sel = v_experts[idx]
        z = jnp.einsum('td,thkd->thk', xc, u_sel)
        a = (jax.nn.gelu(z.astype(jnp.float32)) * g).astype(xc.dtype)
        return jnp.einsum('thk,thkd->td', a, v_sel)

    out = lax.map(chunk, tokens)
    return out.reshape(B, S, D)

def second_inputs(seed: int = 0) -> dict:
    key = jax.random.key(seed)
    ks = jax.random.split(key, 20)
    f32 = jnp.float32
    D = D_MODEL
    nrm = lambda k, shape, s: jax.random.normal(k, shape, f32) * s
    return {
        "x": nrm(ks[0], (BATCH, SEQ, D), 1.0),
        "c": nrm(ks[1], (BATCH, D), 1.0),
        "w_ada": nrm(ks[2], (DEPTH_2, D, 6 * D), 0.5 * D ** -0.5),
        "b_ada": nrm(ks[3], (DEPTH_2, 6 * D), 0.02),
        "norm1_g": 1.0 + nrm(ks[4], (DEPTH_2, D), 0.02),
        "w_in": nrm(ks[5], (DEPTH_2, D, D_IN), D ** -0.5),
        "sink_a": nrm(ks[6], (DEPTH_2, N_HEADS_A), 0.5),
        "t5_table": nrm(ks[7], (T5_BUCKETS, N_HEADS_A), 0.3),
        "rpb_b": nrm(ks[8], (DEPTH_2, N_HEADS_B, 2 * NA_ROWS - 1, 2 * NA_COLS - 1), 0.3),
        "out_norm_a": 1.0 + nrm(ks[9], (DEPTH_2, W_QA), 0.02),
        "out_norm_b": 1.0 + nrm(ks[10], (DEPTH_2, W_B), 0.02),
        "w_out": nrm(ks[11], (DEPTH_2, D_MIX, D), D_MIX ** -0.5),
        "norm2_g": 1.0 + nrm(ks[12], (DEPTH_2, D), 0.02),
        "w_query": nrm(ks[13], (DEPTH_2, D, PEER_HEADS * PEER_QDIM), D ** -0.5),
        "sub_keys": nrm(ks[14], (DEPTH_2, PEER_HEADS, 2, PEER_KEYS, PEER_HALF), PEER_HALF ** -0.5),
        "u_experts": nrm(ks[15], (DEPTH_2, N_EXPERTS, D), D ** -0.5),
        "v_experts": nrm(ks[16], (DEPTH_2, N_EXPERTS, D), 1.0),
        "final_g": 1.0 + nrm(ks[17], (D,), 0.02),
    }

def second_block(x, c, w_ada, b_ada, norm1_g, w_in, sink_a, t5_table, rpb_b, out_norm_a, out_norm_b,
              w_out, norm2_g, w_query, sub_keys, u_experts, v_experts, final_g):
    B, S, D = x.shape
    c_act = jax.nn.silu(c)
    for layer in range(DEPTH_2):
        ada = c_act @ w_ada[layer] + b_ada[layer]
        shift1, scale1, gate1, shift2, scale2, gate2 = jnp.split(ada, 6, axis=-1)

        h = modulate(rms_norm(x, norm1_g[layer]), shift1, scale1)
        proj = h @ w_in[layer]
        qa, ka, va, qb, kb, vb = jnp.split(proj, IN_SPLITS, axis=-1)
        o_a = windowed_gqa(qa.reshape(B, S, N_HEADS_A, HEAD_DIM),
                           ka.reshape(B, S, N_KV_A, HEAD_DIM),
                           va.reshape(B, S, N_KV_A, HEAD_DIM),
                           sink_a[layer], t5_table)
        o_b = neighbourhood_attention(qb.reshape(B, S, N_HEADS_B, HEAD_DIM),
                                      kb.reshape(B, S, N_HEADS_B, HEAD_DIM),
                                      vb.reshape(B, S, N_HEADS_B, HEAD_DIM),
                                      rpb_b[layer])
        mixed = jnp.concatenate([rms_norm(o_a, out_norm_a[layer]),
                                 rms_norm(o_b, out_norm_b[layer])], axis=-1)
        x = x + gate1[:, None, :] * (mixed @ w_out[layer])

        h2 = modulate(rms_norm(x, norm2_g[layer]), shift2, scale2)
        x = x + gate2[:, None, :] * peer(h2, w_query[layer], sub_keys[layer],
                                          u_experts[layer], v_experts[layer])
    return rms_norm(x, final_g)


def setup_inputs(seed=0):
    out = dict(first_inputs(seed))
    for name, value in second_inputs(seed + 1).items():
        if name != "x":
            out[name + "_2"] = value
    return out


def reference(
    x, norm_mix, w_in, conv_w, w_attn_out, w_conv_out, w_mix_out, norm_mlp, w_mlp_up,
    w_mlp_down, norm_final, c_2, w_ada_2, b_ada_2, norm1_g_2, w_in_2, sink_a_2, t5_table_2,
    rpb_b_2, out_norm_a_2, out_norm_b_2, w_out_2, norm2_g_2, w_query_2, sub_keys_2, u_experts_2,
    v_experts_2, final_g_2,
):
    x = first_block(
        x, norm_mix, w_in, conv_w, w_attn_out, w_conv_out, w_mix_out, norm_mlp, w_mlp_up,
        w_mlp_down, norm_final,
    )
    return second_block(
        x, c_2, w_ada_2, b_ada_2, norm1_g_2, w_in_2, sink_a_2, t5_table_2, rpb_b_2,
        out_norm_a_2, out_norm_b_2, w_out_2, norm2_g_2, w_query_2, sub_keys_2, u_experts_2,
        v_experts_2, final_g_2,
    )


_drawn_inputs = setup_inputs


def setup_inputs(seed=0):
    import zlib

    import numpy as np

    out = dict(_drawn_inputs(seed))
    spreads = {}
    factors = {'norm1_g_2': 4.387,
     'sink_a_2': 64.0,
     'out_norm_a_2': 58.667,
     'out_norm_b_2': 51.328,
     'final_g_2': 23.235,
     'norm2_g_2': 13.419}
    for name, (base, spread) in spreads.items():
        noise = np.random.default_rng([zlib.crc32(name.encode()), seed]).standard_normal(out[name].shape)
        drawn = base * np.exp(spread * noise) if base else spread * noise
        out[name] = __import__('jax').numpy.asarray(drawn.astype(out[name].dtype))
    for name, factor in factors.items():
        out[name] = (out[name] * factor).astype(out[name].dtype)
    return out
```

```python
import numpy as np
from contextlib import ExitStack

import concourse.bass as bass
from concourse import mybir

F32 = mybir.dt.float32
F32R = mybir.dt.float32r
U32 = mybir.dt.uint32
ALU = mybir.AluOpType
ACT = mybir.ActivationFunctionType
AX = mybir.AxisListType
ENG = mybir.EngineType

P = 128
T, D = 256, 1024
NT, KD = T // P, D // P
LAYERS = 2
H, DH = 8, 64
W = H * DH
KW = W // P
IH = 4
TOPK = T // 4
CHUNK = 64
TAPS = 3
HID = 4 * D
KH = HID // P
ROPE, ROPE_THETA = DH // 4, 500000.0
EPS = 1e-6
WINDOW, T5_BUCKETS, T5_MAX = 128, 32, 128
GRID_W, NA_ROWS, NA_COLS = 64, 8, 16
ROWS = T // GRID_W
PH, PK, PT = 8, 128, 16
BIAS_W = T + P
T5_W = BIAS_W + P
NA_DR = 2 * ROWS - 1
BIG = 1e30
OUT_OF_BLOCK = -3.0e38
TAKEN = -3.4e38

PIECE = 1024
RING = 4
AHEAD = 3
N_LAYER = 60 + 2 * KH
N_ADA = 6 * KD
N_MIXER2 = 18 + KD
N_QUERY = 2 * PH
N_PIECES = LAYERS * N_LAYER + N_ADA + N_MIXER2 + N_QUERY + 2 * PK
SEL_PIECES = 12
assert N_LAYER % RING == 0 and N_ADA % RING == 0


class Line:

    def __init__(self, eng, sem):
        self.eng, self.sem, self.n, self.seen = eng, sem, 0, {}

    def wait(self, *marks):
        for mark in marks:
            if mark is None:
                continue
            sem, value = mark
            if isinstance(value, int):
                if self.seen.get(sem.name, 0) >= value:
                    continue
                self.seen[sem.name] = value
            self.eng.wait_ge(sem, value)

    def done(self, instruction):
        instruction.then_inc(self.sem, 1)
        self.n += 1
        return self.sem, self.n

    def go(self, marks, method, *args, **kw):
        self.wait(*marks)
        return self.done(method(*args, **kw))

    def restart(self):
        self.n, self.seen = 0, {}


def build(nc, stream, x_in, gains1, gains2, conv_w, b_ada, c_cols, kept_in, rope_in, na_mask_in,
          t5_in, t5_hot, rpb_pad, sinks, sub_keys, gain_out, out):
    ctx = ExitStack()
    with ctx:
        def sb(c, name, shape, dt=F32):
            return c.enter_context(nc.sbuf_tensor(name, shape, dt))

        def sem(name):
            return ctx.enter_context(nc.semaphore(name))

        t5_dram = nc.dram_tensor("t5_by_distance", [1, H * T5_W], F32, kind="Internal").ap()
        t5_rows = nc.dram_tensor("t5_rows", [P, H * T5_W], F32, kind="Internal").ap()
        rpb_rows = nc.dram_tensor("rpb_rows", [GRID_W, H * NA_DR * P], F32, kind="Internal").ap()
        x_dram = nc.dram_tensor("x_parked", [NT, P, D], F32, kind="Internal").ap()
        gate_dram = nc.dram_tensor("gate2_parked", [1, D], F32, kind="Internal").ap()

        raw = sb(ctx, "raw", [P, RING, PIECE])
        w_hi = sb(ctx, "w_hi", [P, RING, PIECE], F32R)
        w_lo = sb(ctx, "w_lo", [P, RING, PIECE], F32R)
        u_hi = sb(ctx, "u_hi", [P, KD, T], F32R)
        u_lo = sb(ctx, "u_lo", [P, KD, T], F32R)
        a_hi = sb(ctx, "a_hi", [P, 2, T], F32R)
        a_lo = sb(ctx, "a_lo", [P, 2, T], F32R)
        kept = sb(ctx, "kept", [P, 2 * P + PT])
        ident, iota, iota16 = kept[:, 0:P], kept[:, P:2 * P], kept[:, 2 * P:2 * P + PT]
        st = sb(ctx, "st", [P, 10, NT])
        bank = [ctx.enter_context(nc.psum_tensor(f"bank{i}", [P, 512], F32)) for i in range(8)]

        landed = [sem(f"landed{i}") for i in range(RING)]
        s_hi = sem("s_hi")
        s_split = sem("s_split")
        s_used = sem("s_used")
        s_relu = sem("s_relu")
        s_act = sem("s_act")
        s_kept, s_x, s_gain, s_cw, s_rope, s_c = (sem(n) for n in (
            "s_kept", "s_x", "s_gain", "s_cw", "s_rope", "s_c"))
        s_t5, s_t5w, s_t5b, s_na, s_gain2, s_bada, s_sink, s_naw, s_sk = (sem(n) for n in (
            "s_t5", "s_t5w", "s_t5b", "s_na", "s_gain2", "s_bada", "s_sink", "s_naw", "s_sk"))
        s_park, s_back, s_out = sem("s_park"), sem("s_back"), sem("s_out")
        s_d = sem("s_d")
        s_z, s_chain, s_ha, s_hb, s_g, s_m, s_ah, s_al = (sem(n) for n in (
            "s_z", "s_chain", "s_ha", "s_hb", "s_g", "s_m", "s_ah", "s_al"))
        PE = Line(nc.tensor, sem("s_pe"))
        AC = Line(nc.scalar, sem("s_ac"))
        VE = Line(nc.vector, sem("s_ve"))
        PO = Line(nc.gpsimd, sem("s_po"))
        lines = (PE, AC, VE, PO)
        compute = bass.OrderedEngineSet([ENG.PE, ENG.Activation, ENG.DVE, ENG.Pool])
        V, S, M, G = nc.vector, nc.scalar, nc.tensor, nc.gpsimd

        nc.sync.dma_start(kept[:, :], kept_in).then_inc(s_kept, 16)
        for s in range(RING):
            nc.sync.dma_start(raw[:, s, :], stream[s]).then_inc(landed[s], 16)
        def load_piece(i, s):
            nc.sync.wait_ge(s_split, i * RING + (s + 1 - RING))
            nc.sync.dma_start(raw[:, s, :], stream[bass.ds(i * RING + s, 1), :, :].rearrange(
                "a p n -> (a p) n")).then_inc(landed[s], 16)
        with nc.sync.Fori(1, N_PIECES // RING) as i:
            for s in range(RING):
                load_piece(i, s)
        for s in range(N_PIECES % RING):
            load_piece(N_PIECES // RING, s)

        at = {"piece": 0, "quads": 0}

        def dyn(k):
            return at["quads"] * k

        def split(c):
            s = c % RING
            nc.scalar.wait_ge(landed[s], dyn(16) + 16 * (c // RING + 1))
            if c >= RING:
                nc.scalar.wait_ge(s_used, dyn(RING) + (c - RING + 1))
            nc.scalar.activation(w_hi[:, s, :], raw[:, s, :], ACT.Copy).then_inc(s_hi, 1)
            nc.vector.wait_ge(s_hi, dyn(RING) + (c + 1))
            nc.vector.tensor_tensor(w_lo[:, s, :], raw[:, s, :], w_hi[:, s, :].bitcast(F32),
                                    ALU.subtract).then_inc(s_split, 1)

        def next_piece(last=False):
            c = at["piece"]
            at["piece"] = c + 1
            if not last:
                split(c + AHEAD)
            nc.tensor.wait_ge(s_split, dyn(RING) + (c + 1))
            return c % RING

        def used(instruction):
            instruction.then_inc(s_used, 1)
            return s_used, dyn(RING) + at["piece"]

        def mm3(o, lh, ll, rh, rl, start, stop):
            M.matmul(o, lh, rh, start=start, stop=False, skip_group_check=True)
            M.matmul(o, lh, rl, start=False, stop=False, skip_group_check=True)
            return M.matmul(o, ll, rh, start=False, stop=stop, skip_group_check=True)

        def piece_b(o, rhs_hi, rhs_lo, kt=KD, parts=1, last=False):
            s = next_piece(last)
            for part in range(parts):
                for k in range(kt):
                    col = (part * kt + k) * P
                    i = mm3(o[part], w_hi[:, s, col:col + P], w_lo[:, s, col:col + P],
                            rhs_hi[:, k, :], rhs_lo[:, k, :], k == 0, k == kt - 1)
            return used(i)

        def piece_a(o, lhs, ks, width, first, final):
            s = next_piece()
            for j, k in enumerate(ks):
                for tt in range(NT):
                    lh, ll = (u[:, k, tt * P:(tt + 1) * P] for u in lhs)
                    for n in range(width // 512):
                        col = j * width + n * 512
                        i = mm3(o[tt][n], lh, ll, w_hi[:, s, col:col + 512],
                                w_lo[:, s, col:col + 512], first and j == 0,
                                final and j == len(ks) - 1)
            return used(i)

        free = {}

        def take(i):
            PE.wait(*free.get(i, ()))

        def restart_lines():
            nc.multi_engine_barrier(compute)
            for line in lines:
                line.eng.sem_clear(line.sem)
                line.restart()
            nc.multi_engine_barrier(compute)
            free.clear()

        def transposes(b, sources, marks):
            take(b)
            PE.wait(*marks)
            for j, src in enumerate(sources):
                i = M.transpose(bank[b][:, j * P:(j + 1) * P], src, ident)
            return PE.done(i)

        def split_bank(src, hi, lo, mark, extra=()):
            m = AC.go((mark, *extra), S.activation, hi, src, ACT.Copy)
            return VE.go((m, mark), V.tensor_tensor, lo, src, hi.bitcast(F32), ALU.subtract), m

        def row_scale(tt, src, width, slot, junk, marks):
            c = [st[:, slot + j, tt:tt + 1] for j in range(5)]
            m = AC.go(marks, S.activation, junk, src, ACT.Square, accum_out=c[0])
            m = VE.go((m,), V.tensor_scalar, c[1], c[0], 1.0 / width, EPS, ALU.mult, ALU.add)
            m = VE.go((m,), V.reciprocal, c[2], c[1])
            m = AC.go((m,), S.activation, c[3], c[2], ACT.Sqrt)
            m = VE.go((m,), V.tensor_tensor, c[4], c[3], c[3], ALU.mult)
            m = VE.go((m,), V.tensor_tensor, c[4], c[4], c[1], ALU.mult)
            m = VE.go((m,), V.tensor_scalar, c[4], c[4], -0.5, 1.5, ALU.mult, ALU.add)
            return c[4], c[3], VE.go((m,), V.tensor_tensor, c[4], c[4], c[3], ALU.mult)

        def norm_to_u(x, xn, gain, marks, u_free, shift=None):
            last = []
            for tt in range(NT):
                r, _, m = row_scale(tt, x[:, tt, :], D, 0, xn[:, tt, :], marks)
                m = VE.go((m,), V.scalar_tensor_tensor, xn[:, tt, :], x[:, tt, :], r, gain,
                          ALU.mult, ALU.mult)
                if shift is not None:
                    m = VE.go((m,), V.tensor_tensor, xn[:, tt, :], xn[:, tt, :], shift, ALU.add)
                for g in range(KD // 4):
                    b = 6 + g % 2
                    t = transposes(b, [xn[:, tt, k * P:(k + 1) * P] for k in range(4 * g, 4 * g + 4)],
                                   (m,))
                    cols = slice(tt * P, (tt + 1) * P)
                    m2, m1 = split_bank(bank[b][:, :].rearrange("p (k n) -> p k n", k=4),
                                        u_hi[:, 4 * g:4 * g + 4, cols],
                                        u_lo[:, 4 * g:4 * g + 4, cols], t, u_free)
                    free[b] = (m1, m2)
                last += [m1, m2]
            PE.wait(*last)
            return last

        def add_to_x(x, marks):
            out_marks = []
            for tt in range(NT):
                for n in range(2):
                    b = 2 * tt + n
                    cols = x[:, tt, n * 512:(n + 1) * 512]
                    m = VE.go(marks, V.tensor_tensor, cols, cols, bank[b][:, :], ALU.add)
                    free[b] = (m,)
                    out_marks.append(m)
            return out_marks[-1]

        def acc_banks():
            for b in range(4):
                take(b)
            return [[bank[0][:, :], bank[1][:, :]], [bank[2][:, :], bank[3][:, :]]]

        SAME_GROUP = [slice(h, h + 2) for h in range(0, H, 2)]
        SAME_PARITY = [slice(h, h + 3, 2) for h in (0, 1, 4, 5)]

        def attention(tt, nk, q, k, v, bias, bias_mark, buf, o, marks, pairs, sink=None):
            p, pt = buf["p"], buf["pt"]
            mx, nm, sm, ri, es = (buf["rows"][:, j, :] for j in range(5))
            for hp in range(H // 2):
                take(hp)
                PE.wait(*marks)
                for e, h in enumerate(range(H)[pairs[hp]]):
                    i = M.matmul(bank[hp][:, e * nk:(e + 1) * nk], q(h), k(h), start=True, stop=True,
                                 skip_group_check=True)
                m = PE.done(i)
                m = VE.go((m, *bias_mark, buf.get("p_free")), V.scalar_tensor_tensor,
                          p[:, pairs[hp], 0:nk],
                          bank[hp][:, 0:2 * nk].rearrange("p (a n) -> p a n", a=2),
                          DH ** -0.5, bias(pairs[hp]), ALU.mult, ALU.add)
                free[hp] = (m,)
                if hp % 2:
                    yield
            if sink is None:
                m = VE.go((m,), V.tensor_reduce, nm, p[:, :, 0:nk], AX.X, ALU.max, negate=True)
            else:
                m = VE.go((m,), V.tensor_reduce, mx, p[:, :, 0:nk], AX.X, ALU.max)
                m = VE.go((m,), V.tensor_tensor, mx, mx, sink, ALU.max)
                m = VE.go((m,), V.tensor_scalar, nm, mx, -1.0, None, ALU.mult)
                m = VE.go((m,), V.tensor_tensor, es, sink, nm, ALU.add)
            yield
            if sink is not None:
                e_m = AC.go((m,), S.activation, es, es, ACT.Exp)
            for h in range(H):
                m1 = AC.go((m,), S.activation, p[:, h, 0:nk], p[:, h, 0:nk], ACT.Exp,
                           bias=nm[:, h:h + 1], accum_out=sm[:, h:h + 1])
                if h % 3 == 2:
                    yield
            if sink is not None:
                m = VE.go((m1, e_m), V.tensor_tensor, sm, sm, es, ALU.add)
                m = VE.go((m,), V.reciprocal, ri, sm)
            else:
                m = VE.go((m1,), V.reciprocal, ri, sm)
            yield
            n = 0
            for kt in range(nk // P):
                for g in range(2):
                    b = 6 + n % 2
                    t = transposes(b, [p[:, h, kt * P:(kt + 1) * P] for h in range(4 * g, 4 * g + 4)],
                                   (m1,))
                    dst = pt[:, kt, 4 * g:4 * g + 4, :]
                    src = bank[b][:, :].rearrange("p (h n) -> p h n", h=4)
                    if n % 2:
                        e1 = VE.go((t, buf.get("pt_free")), V.tensor_copy, dst, src)
                    else:
                        e1 = AC.go((t, buf.get("pt_free")), S.activation, dst, src, ACT.Copy)
                    free[b] = (e1,)
                    PE_marks = buf.setdefault("pt_marks", {})
                    PE_marks[n] = e1
                    n += 1
                yield
            buf["p_free"] = t
            PE.wait(*buf["pt_marks"].values())
            take(6)
            for h in range(H):
                for kt in range(nk // P):
                    i = M.matmul(bank[6][:, h * DH:(h + 1) * DH], pt[:, kt, h, :], v(kt, h),
                                 start=kt == 0, stop=kt == nk // P - 1, skip_group_check=True)
            t = PE.done(i)
            buf["pt_free"] = t
            yield
            m = VE.go((t, m), V.tensor_tensor, o.rearrange("p (h d) -> p h d", h=H),
                      bank[6][:, :].rearrange("p (h d) -> p h d", h=H),
                      ri.unsqueeze(2).to_broadcast([P, H, DH]), ALU.mult)
            free[6] = (m,)
            buf["done"] = m

        def weave(main, side, every=1):
            for n, _ in enumerate(main):
                for _ in range(every):
                    next(side, None)
            for _ in side:
                pass

        ph1 = ctx.enter_context(ExitStack())
        x = sb(ph1, "x", [P, NT, D])
        xn = sb(ph1, "xn", [P, NT, D])
        buf = {"p": sb(ph1, "p", [P, H, T]), "pt": sb(ph1, "pt", [P, NT, H, P]),
               "rows": sb(ph1, "rows", [P, 5, H])}
        o_sb = sb(ph1, "o_sb", [P, NT, W])
        qT, kT = sb(ph1, "qT", [P, KW, T]), sb(ph1, "kT", [P, KW, T])
        v_sb = sb(ph1, "v_sb", [P, NT, W])

        ph1a = ph1.enter_context(ExitStack())
        gains = sb(ph1a, "gains", [P, 2 * LAYERS, D])
        rope = sb(ph1a, "rope", [P, 2, 2 * T])
        turn = sb(ph1a, "turn", [P, P])
        cw_all = sb(ph1a, "cw_all", [P, LAYERS, KW * TAPS])
        cw = sb(ph1a, "cw", [P, KW, TAPS])
        gate = sb(ph1a, "gate", [P, 2 * KD, T])
        iqT, ikT = sb(ph1a, "iqT", [P, 2, T]), sb(ph1a, "ikT", [P, T])
        iwT, iw = sb(ph1a, "iwT", [P, T]), sb(ph1a, "iw", [P, NT, IH])
        work = sb(ph1a, "work", [P, 2, T])
        score, sbias = sb(ph1a, "score", [P, NT, T]), sb(ph1a, "sbias", [P, NT, T])
        top8 = sb(ph1a, "top8", [P, 8])
        rot = sb(ph1a, "rot", [P, 2, 2 * T])
        cc = sb(ph1a, "cc", [P, 2, 2 * T])
        prod = sb(ph1a, "prod", [P, KW, T + TAPS - 1])
        yc = sb(ph1a, "yc", [P, KW, T])
        o_hi, o_lo = sb(ph1a, "o_hi", [P, KW, T], F32R), sb(ph1a, "o_lo", [P, KW, T], F32R)
        y_hi, y_lo = sb(ph1a, "y_hi", [P, KW, T], F32R), sb(ph1a, "y_lo", [P, KW, T], F32R)
        relu = sb(ph1a, "relu", [P, 2, T])

        S.dma_start(x[:, :, :], x_in.rearrange("(t p) d -> p t d", p=P)).then_inc(s_x, 16)
        S.dma_start(gains[:, :, :], gains1.partition_broadcast(P)).then_inc(s_gain, 16)
        S.dma_start(rope[:, :, :].rearrange("p a n -> p (a n)"), rope_in[:, 0:4 * T]).then_inc(s_rope, 16)
        S.dma_start(turn[:, :], rope_in[:, 4 * T:4 * T + P]).then_inc(s_rope, 16)
        S.dma_start(cw_all[:, :, :], conv_w).then_inc(s_cw, 16)
        for e in (nc.vector, nc.tensor, nc.scalar, nc.gpsimd):
            e.wait_ge(s_kept, 16)
            e.wait_ge(s_x, 16)
            e.wait_ge(s_gain, 16)
            e.wait_ge(s_rope, 32)
            e.wait_ge(s_cw, 16)
        nc.vector.memset(prod[:, :, 0:TAPS - 1], 0.0)
        for c in range(AHEAD):
            split(c)

        with nc.Fori(0, LAYERS, engines=compute) as layer:
            at["quads"] = layer * (N_LAYER // RING)
            restart_lines()
            buf.pop("p_free", None), buf.pop("pt_free", None)
            norm_to_u(x, xn, gains[:, bass.ds(layer * 1, 1), :].rearrange("p a n -> p (a n)"), (), ())
            cw_m = VE.go((), V.tensor_copy, cw[:, :, :].rearrange("p a b -> p (a b)"),
                         cw_all[:, bass.ds(layer * 1, 1), :].rearrange("p a n -> p (a n)"))
            U = (u_hi, u_lo)
            got = {}

            def main_part():
                take(4)
                m = piece_b([bank[4][:, 0:T]], *U)
                got["iwT"] = AC.go((m,), S.activation, iwT[0:32, :], bank[4][0:32, 0:T], ACT.Copy)
                free[4] = (got["iwT"],)
                yield
                plan = [("iq", iqT, 0, 2), ("ik", ikT, 0, 1), ("k", kT, 0, 2), ("k", kT, 2, 2),
                        ("q", qT, 0, 2), ("q", qT, 2, 2)]
                for n, (name, dst, f, parts) in enumerate(plan):
                    b = 5 - n % 2
                    take(b)
                    for e in range(parts):
                        m = piece_b([bank[b][:, e * T:(e + 1) * T]], *U)
                        if e < parts - 1:
                            yield
                    d = dst[:, :] if name == "ik" else dst[:, f:f + 2, :].rearrange("p a n -> p (a n)")
                    m = AC.go((m,), S.activation, d, bank[b][:, 0:parts * T], ACT.Copy)
                    free[b] = (m,)
                    got[name, f] = m
                    yield
                take(0), take(1)
                for g in range(KD // 2):
                    m = piece_a([[bank[0][:, :]], [bank[1][:, :]]], U, (2 * g, 2 * g + 1), 512,
                                g == 0, g == KD // 2 - 1)
                    if g < KD // 2 - 1:
                        yield
                for tt in range(NT):
                    mv = AC.go((m,), S.activation, v_sb[:, tt, :], bank[tt][:, :], ACT.Copy)
                    free[tt] = (mv,)
                got["v"] = mv
                yield
                for f in (0, 2):
                    for name in ("cC", "ch"):
                        b = 4 if name == "cC" else 5
                        take(b)
                        piece_b([bank[b][:, 0:T]], *U)
                        yield
                        m = piece_b([bank[b][:, T:2 * T]], *U)
                        if name == "cC":
                            mc = AC.go((m, got.get("prod")), S.activation, cc[:, 0, :], bank[b][:, :],
                                       ACT.Copy)
                            free[b] = (mc,)
                        else:
                            m = VE.go((m, mc), V.tensor_tensor, prod[:, f:f + 2, TAPS - 1:],
                                      bank[b][:, :].rearrange("p (a n) -> p a n", a=2),
                                      cc[:, 0, :].rearrange("p (a n) -> p a n", a=2), ALU.mult)
                            got["prod"] = m
                            free[b] = (m,)
                        yield
                for f in (0, 2):
                    b = 4 + f // 2
                    take(b)
                    piece_b([bank[b][:, 0:T]], *U)
                    for ff in (f, f + 1):
                        m = VE.go((got["prod"], cw_m), V.tensor_scalar, yc[:, ff, :],
                                  prod[:, ff, 0:T], cw[:, ff, 0:1], None, ALU.mult)
                        for j in range(1, TAPS):
                            m = VE.go((m,), V.scalar_tensor_tensor, yc[:, ff, :], prod[:, ff, j:j + T],
                                      cw[:, ff, j:j + 1], yc[:, ff, :], ALU.mult, ALU.add)
                    yield
                    m2 = piece_b([bank[b][:, T:2 * T]], *U)
                    dst = yc[:, f:f + 2, :].rearrange("p a n -> p (a n)")
                    m = VE.go((m, m2), V.tensor_tensor, dst, dst, bank[b][:, :], ALU.mult)
                    free[b] = (m,)
                    got["y"] = split_bank(yc[:, f:f + 2, :], y_hi[:, f:f + 2, :],
                                          y_lo[:, f:f + 2, :], m)
                    yield
                for f in range(0, 2 * KD, 2):
                    b = 4 + (f // 2) % 2
                    take(b)
                    piece_b([bank[b][:, 0:T]], *U)
                    yield
                    m = piece_b([bank[b][:, T:2 * T]], *U)
                    m = AC.go((m,), S.activation, gate[:, f:f + 2, :].rearrange("p a n -> p (a n)"),
                              bank[b][:, :], ACT.Sigmoid)
                    free[b] = (m,)
                    got["gate"] = m
                    yield

            def rope_of(name, dst, f, parts, b):
                n = parts * T
                d = dst[:, :] if name == "ik" else dst[:, f:f + 2, :].rearrange("p a n -> p (a n)")
                PE.wait(got[name, f])
                take(b)
                t = PE.done(M.matmul(bank[b][:, 0:n], turn[:, :], d, start=True, stop=True))
                r = rot[:, b - 6, 0:n]
                m = VE.go((t, got.get(("rot", b))), V.tensor_tensor, r, bank[b][:, 0:n],
                          rope[:, 1, 0:n], ALU.mult)
                free[b] = (m,)
                m1 = VE.go((t, got[name, f]), V.tensor_tensor, d, d, rope[:, 0, 0:n], ALU.mult)
                m = VE.go((m, m1), V.tensor_tensor, d, d, r, ALU.add)
                got["rot", b] = m
                got[name, f, "r"] = m

            def side_part():
                for _ in range(4):
                    yield
                take(6)
                PE.wait(got["iwT"])
                for tt in range(NT):
                    i = M.transpose(bank[6][:, tt * 32:tt * 32 + 32], iwT[0:32, tt * P:(tt + 1) * P],
                                    ident[0:32, 0:32])
                t = PE.done(i)
                iw_m = VE.go((t,), V.tensor_scalar, iw[:, :, :],
                             bank[6][:, 0:64].rearrange("p (t n) -> p t n", t=2)[:, :, 0:IH],
                             DH ** -0.5 * IH ** -0.5, None, ALU.mult)
                free[6] = (iw_m,)
                rope_of("iq", iqT, 0, 2, 7)
                yield
                rope_of("ik", ikT, 0, 1, 6)
                yield
                for tt in range(NT):
                    nk = (tt + 1) * P
                    PE.wait(got["iq", 0, "r"], got["ik", 0, "r"])
                    b = (2, 3)
                    for h in range(IH):
                        bb = b[h % 2]
                        if h < 2:
                            take(bb)
                        r0 = (h % 2) * DH
                        i = M.matmul(bank[bb][:, (h // 2) * nk:(h // 2 + 1) * nk],
                                     iqT[r0:r0 + DH, h // 2, tt * P:(tt + 1) * P],
                                     ikT[r0:r0 + DH, 0:nk], start=True, stop=True,
                                     skip_group_check=True)
                    t = PE.done(i)
                    m = t
                    sc = score[:, tt, 0:nk]
                    for h in range(IH):
                        src = bank[b[h % 2]][:, (h // 2) * nk:(h // 2 + 1) * nk]
                        dst = sc if h == 0 else work[:, 0, 0:nk]
                        m = VE.go((m, t, iw_m), V.tensor_scalar, dst, src, 0.0, iw[:, tt, h:h + 1],
                                  ALU.max, ALU.mult)
                        if h:
                            m = VE.go((m,), V.tensor_tensor, sc, sc, work[:, 0, 0:nk], ALU.add)
                    free[b[0]] = free[b[1]] = (m,)
                    yield
                    m = VE.go((m,), V.memset, score[0:CHUNK, tt, nk - CHUNK:nk], OUT_OF_BLOCK)
                    src = sc
                    for r in range(TOPK // 8):
                        m = VE.go((m,), V.max, top8[:, :], src)
                        dst = work[:, r % 2, 0:nk]
                        m = VE.go((m,), V.match_replace, dst, top8[:, :], src, TAKEN)
                        src = dst
                        if r % 2:
                            yield
                    bs = sbias[:, tt, 0:nk]
                    m = VE.go((m,), V.tensor_tensor, bs, src, sc, ALU.not_equal)
                    m = VE.go((m,), V.tensor_scalar, bs, bs, -1.0, BIG, ALU.add, ALU.mult)
                    got["bias", tt] = m
                    yield
                rope_of("k", kT, 0, 2, 7)
                yield
                rope_of("k", kT, 2, 2, 6)
                yield
                rope_of("q", qT, 0, 2, 7)
                yield
                rope_of("q", qT, 2, 2, 6)
                yield
                ready = [got[n, f, "r"] for n in "qk" for f in (0, 2)] + [got["v"]]
                for tt in range(NT):
                    nk = (tt + 1) * P

                    def rows(tensor, h, cols):
                        return tensor[(h % 2) * DH:(h % 2 + 1) * DH, h // 2, cols]
                    yield from attention(
                        tt, nk, lambda h: rows(qT, h, slice(tt * P, (tt + 1) * P)),
                        lambda h: rows(kT, h, slice(0, nk)),
                        lambda kt, h: v_sb[:, kt, h * DH:(h + 1) * DH],
                        lambda heads: sbias[:, tt, 0:nk].unsqueeze(1).to_broadcast([P, 2, nk]),
                        (got["bias", tt],), buf, o_sb[:, tt, :], ready, SAME_PARITY)
                    yield
                    t = transposes(7, [o_sb[:, tt, k * P:(k + 1) * P] for k in range(KW)],
                                   (buf["done"],))
                    cols = slice(tt * P, (tt + 1) * P)
                    m2, m1 = split_bank(bank[7][:, :].rearrange("p (k n) -> p k n", k=KW),
                                        o_hi[:, :, cols], o_lo[:, :, cols], t)
                    free[7] = (m1, m2)
                    got["o"] = (m1, m2)
                    yield

            weave(main_part(), side_part())
            u_read = (s_used, dyn(RING) + at["piece"])
            PE.wait(*got["o"], *got["y"])
            for g in range(KD // 2):
                pb = 4 + g % 2
                pc = 6 + g % 2
                take(pb)
                ma = piece_b([bank[pb][:, 0:T], bank[pb][:, T:2 * T]], o_hi, o_lo, KW, 2)
                take(pc)
                mc = piece_b([bank[pc][:, 0:T], bank[pc][:, T:2 * T]], y_hi, y_lo, KW, 2)
                e = g % 2
                g0 = gate[:, 2 * g:2 * g + 2, :].rearrange("p a n -> p (a n)")
                g1 = gate[:, KD + 2 * g:KD + 2 * g + 2, :].rearrange("p a n -> p (a n)")
                m = VE.go((ma, got["gate"], got.get(("cc", e))), V.tensor_tensor, cc[:, e, :], bank[pb][:, :], g0,
                          ALU.mult)
                free[pb] = (m,)
                m1 = VE.go((mc,), V.tensor_tensor, rot[:, e, :], bank[pc][:, :], g1, ALU.mult)
                free[pc] = (m1,)
                m = VE.go((m, m1), V.tensor_tensor, cc[:, e, :], cc[:, e, :], rot[:, e, :], ALU.add)
                m2, m1 = split_bank(cc[:, e, :].rearrange("p (a n) -> p a n", a=2),
                                    u_hi[:, 2 * g:2 * g + 2, :], u_lo[:, 2 * g:2 * g + 2, :], m,
                                    (u_read,) if g == 0 else ())
                got["cc", e] = m1
                if g % 2:
                    PE.wait(m1, m2) if g == KD // 2 - 1 else None
            acc = acc_banks()
            for k in range(KD):
                m = piece_a(acc, U, (k,), D, k == 0, k == KD - 1)
            m = add_to_x(x, (m,))
            norm_to_u(x, xn, gains[:, bass.ds(layer * 1 + LAYERS, 1), :].rearrange("p a n -> p (a n)"),
                      (m,), ())
            acc = acc_banks()
            take(4), take(5)

            def up(q, tile, first=False):
                if not first:
                    nc.tensor.wait_ge(s_act, (tile - 2) * 3 + 1)
                m = piece_b([bank[4 + q][:, 0:T]], *U)
                nc.scalar.wait_ge(*m)
                if not first:
                    nc.scalar.wait_ge(s_act, (tile - 2) * 3 + 3)
                nc.scalar.activation(relu[:, q, :], bank[4 + q][:, 0:T], ACT.Relu).then_inc(s_relu, 1)
                nc.vector.wait_ge(s_relu, tile + 1)
                nc.vector.tensor_tensor(relu[:, q, :], relu[:, q, :], bank[4 + q][:, 0:T],
                                        ALU.mult).then_inc(s_act, 1)
                nc.vector.wait_ge(s_act, tile * 3 + 1)
                if not first:
                    nc.vector.wait_ge(s_used, m[1] + 1)
                nc.vector.tensor_copy(a_hi[:, q, :], relu[:, q, :]).then_inc(s_act, 1)
                nc.vector.wait_ge(s_act, tile * 3 + 2)
                nc.vector.tensor_tensor(a_lo[:, q, :], relu[:, q, :], a_hi[:, q, :].bitcast(F32),
                                        ALU.subtract).then_inc(s_act, 1)

            def down(q, tile, first, last):
                nc.tensor.wait_ge(s_act, tile * 3 + 3)
                s = next_piece()
                for tt in range(NT):
                    for n in range(2):
                        i = mm3(acc[tt][n], a_hi[:, q, tt * P:(tt + 1) * P],
                                a_lo[:, q, tt * P:(tt + 1) * P], w_hi[:, s, n * 512:(n + 1) * 512],
                                w_lo[:, s, n * 512:(n + 1) * 512], first, last)
                return used(i)

            tile0 = layer * KH
            up(0, tile0 + 0, True)
            up(1, tile0 + 1, True)
            for q in range(2):
                up(q, tile0 + 2 + q)
                down(q, tile0 + q, q == 0, False)
            base = at["piece"]
            quads = at["quads"]
            with nc.Fori(0, KH // 2 - 2, engines=compute) as i:
                at["quads"] = quads + i
                for q in range(2):
                    up(q, tile0 + i * 2 + (4 + q))
                    down(q, tile0 + i * 2 + (2 + q), False, False)
            at["quads"], at["piece"] = quads, base + (KH - 4) * 2
            for q in range(2):
                m = down(q, tile0 + KH - 2 + q, False, q == 1)
            m = add_to_x(x, (m,))
            assert at["piece"] == N_LAYER
        at["quads"], at["piece"] = 0, LAYERS * N_LAYER
        restart_lines()
        ph1a.close()

        ph1b = ph1.enter_context(ExitStack())
        gains_b = sb(ph1b, "gains_b", [P, 4, D])
        ada = sb(ph1b, "ada", [P, 6, D])
        ccol = sb(ph1b, "ccol", [P, 3, KD])
        c_rep = xn[:, 0, :].rearrange("p (k n) -> p k n", k=KD)
        c_hi, c_lo = sb(ph1b, "c_hi", [P, KD, P], F32R), sb(ph1b, "c_lo", [P, KD, P], F32R)
        t5 = sb(ph1b, "t5", [DH, H])
        hot = sb(ph1b, "hot", [DH, T5_W])
        t5_row = sb(ph1b, "t5_row", [H, T5_W])
        bias_a, bias_b = sb(ph1b, "bias_a", [P, H, BIAS_W]), sb(ph1b, "bias_b", [P, H, BIAS_W])
        na_mask = sb(ph1b, "na_mask", [P, GRID_W])
        sink = sb(ph1b, "sink", [P, H])
        kaT, vaT = sb(ph1b, "kaT", [P, T]), sb(ph1b, "vaT", [P, T])
        va = sb(ph1b, "va", [P, NT, P])
        qbT = sb(ph1b, "qbT", [P, KW, T])
        ob_sb = sb(ph1b, "ob_sb", [P, NT, W])

        S.dma_start(ccol[:, 0, :], c_cols).then_inc(s_c, 16)
        S.dma_start(ada[:, :, :], b_ada.partition_broadcast(P)).then_inc(s_bada, 16)
        S.dma_start(gains_b[:, :, :], gains2.partition_broadcast(P)).then_inc(s_gain2, 16)
        S.dma_start(t5[:, :], t5_in).then_inc(s_t5, 16)
        S.dma_start(hot[:, :], t5_hot).then_inc(s_t5, 16)
        S.dma_start(na_mask[:, :], na_mask_in).then_inc(s_na, 16)
        S.dma_start(sink[:, :], sinks.partition_broadcast(P)).then_inc(s_sink, 16)
        S.dma_start(rpb_rows, rpb_pad.partition_broadcast(GRID_W).rearrange("p a n -> p (a n)")
                    ).then_inc(s_naw, 16)
        S.wait_ge(s_naw, 16)
        row = H * NA_DR * P
        for half in range(2):
            for h in range(H):
                S.dma_start(
                    bias_b[half * GRID_W:(half + 1) * GRID_W, h, :].rearrange("p (q c) -> p q c", c=GRID_W),
                    bass.AP(tensor=rpb_rows.tensor, offset=(h * NA_DR + 1 - half) * P + GRID_W - 1,
                            ap=[[row - 1, GRID_W], [P, BIAS_W // GRID_W], [1, GRID_W]])).then_inc(s_na, 16)
        m = AC.go(((s_c, 16),), S.activation, ccol[:, 1, :], ccol[:, 0, :], ACT.Sigmoid)
        m = VE.go((m, (s_c, 16)), V.tensor_tensor, ccol[:, 2, :], ccol[:, 1, :], ccol[:, 0, :], ALU.mult)
        m = VE.go((m,), V.tensor_copy, c_rep[:, :, :], ccol[:, 2, :].unsqueeze(2).to_broadcast([P, KD, P]))
        c_marks = split_bank(c_rep[:, :, :], c_hi[:, :, :], c_lo[:, :, :], m)
        PE.wait((s_t5, 32))
        t = PE.done(M.matmul(bank[7][0:H, :], t5[:, :], hot[:, :], start=True, stop=True))
        m = VE.go((t,), V.tensor_copy, t5_row[:, :], bank[7][0:H, :])
        free[7] = (m,)
        AC.wait(m)
        S.dma_start(t5_dram.rearrange("a (h n) -> (a h) n", h=H), t5_row[:, :]).then_inc(s_t5w, 16)
        S.wait_ge(s_t5w, 16)
        S.dma_start(t5_rows, t5_dram.partition_broadcast(P).rearrange("p a n -> p (a n)")).then_inc(s_t5w, 16)
        S.wait_ge(s_t5w, 32)
        S.dma_start(bias_a[:, :, :], bass.AP(tensor=t5_rows.tensor, offset=P - 1,
                                             ap=[[H * T5_W - 1, P], [T5_W, H], [1, BIAS_W]])
                    ).then_inc(s_t5b, 16)
        bb = bias_b[:, :, :].rearrange("p h (q c) -> p (h q) c", c=GRID_W)
        nb_mark = VE.go(((s_na, 16 * (1 + 2 * H)),), V.tensor_tensor, bb, bb,
                        na_mask[:, :].unsqueeze(1).to_broadcast([P, H * BIAS_W // GRID_W, GRID_W]), ALU.add)

        def ada_group(g):
            PE.wait(*c_marks)
            b = (4, 5)
            take(b[0]), take(b[1])
            for k in range(KD):
                s = next_piece()
                for n in range(2):
                    i = mm3(bank[b[n]][:, :], c_hi[:, k, :], c_lo[:, k, :],
                            w_hi[:, s, n * 512:(n + 1) * 512], w_lo[:, s, n * 512:(n + 1) * 512],
                            k == 0, k == KD - 1)
                m = used(i)
                if k < KD - 1:
                    yield
            for n in range(2):
                cols = ada[:, g, n * 512:(n + 1) * 512]
                mm = VE.go((m, (s_bada, 16)), V.tensor_tensor, cols, cols, bank[b[n]][:, :], ALU.add)
                free[b[n]] = (mm,)
            got["ada", g] = mm
            yield

        for tt in range(NT):
            r, _, m = row_scale(tt, x[:, tt, :], D, 0, xn[:, tt, :], c_marks)
            VE.go((m, (s_gain2, 16)), V.scalar_tensor_tensor, x[:, tt, :], x[:, tt, :], r,
                  gains_b[:, 0, :], ALU.mult, ALU.mult)
        got = {}
        for g in range(2):
            for _ in ada_group(g):
                pass
        m = VE.go((got["ada", 1], (s_gain2, 16)), V.scalar_tensor_tensor, ada[:, 1, :], ada[:, 1, :], 1.0,
                  gains_b[:, 1, :], ALU.add, ALU.mult)
        norm_to_u(x, xn, ada[:, 1, :], (m,), (), ada[:, 0, :])
        U = (u_hi, u_lo)
        buf.pop("p_free", None), buf.pop("pt_free", None)

        def main2():
            plan = [(kaT, None, 1, "ka"), (qT, 0, 2, "qa"), (qT, 2, 2, "qa"), (vaT, None, 1, "va"),
                    (kT, 0, 2, "kb"), (kT, 2, 2, "kb"), (qbT, 0, 2, "qb"), (qbT, 2, 2, "qb")]
            for n, (dst, f, parts, name) in enumerate(plan):
                b = 4 + n % 2
                take(b)
                for e in range(parts):
                    m = piece_b([bank[b][:, e * T:(e + 1) * T]], *U)
                    if e < parts - 1:
                        yield
                d = dst[:, :] if f is None else dst[:, f:f + 2, :].rearrange("p a n -> p (a n)")
                m = AC.go((m,), S.activation, d, bank[b][:, 0:parts * T], ACT.Copy)
                free[b] = (m,)
                got[name] = m
                yield
            take(4), take(5)
            for g in range(KD // 2):
                m = piece_a([[bank[4][:, :]], [bank[5][:, :]]], U, (2 * g, 2 * g + 1), 512,
                            g == 0, g == KD // 2 - 1)
                if g < KD // 2 - 1:
                    yield
            for tt in range(NT):
                mv = AC.go((m,), S.activation, v_sb[:, tt, :], bank[4 + tt][:, :], ACT.Copy)
                free[4 + tt] = (mv,)
            got["vb"] = mv
            got["u_read"] = m
            yield
            for g in range(2, 6):
                yield from ada_group(g)

        def mixed(tt, src, k0, cols):
            r, _, m = row_scale(tt, src[:, tt, :], W, 5, xn[:, tt, 0:W], (buf["done"],))
            m = VE.go((m, (s_gain2, 16)), V.scalar_tensor_tensor, src[:, tt, :], src[:, tt, :], r,
                      gains_b[:, 3, cols], ALU.mult, ALU.mult)
            yield
            t = transposes(7, [src[:, tt, k * P:(k + 1) * P] for k in range(KW)], (m,))
            rows = slice(tt * P, (tt + 1) * P)
            m2, m1 = split_bank(bank[7][:, :].rearrange("p (k n) -> p k n", k=KW),
                                u_hi[:, k0:k0 + KW, rows], u_lo[:, k0:k0 + KW, rows], t,
                                (got["u_read"],))
            free[7] = (m1, m2)
            got["mix"] = (m1, m2)
            yield

        def side2():
            for _ in range(7):
                yield
            take(7)
            PE.wait(got["va"])
            for tt in range(NT):
                i = M.transpose(bank[7][:, tt * P:(tt + 1) * P], vaT[:, tt * P:(tt + 1) * P], ident)
            t = PE.done(i)
            va_mark = VE.go((t,), V.tensor_copy, va[:, :, :].rearrange("p a n -> p (a n)"),
                            bank[7][:, 0:NT * P])
            free[7] = (va_mark,)

            def bias_of(table, tt):
                return lambda heads: table[:, heads, P * (1 - tt):P * (1 - tt) + T]
            for tt in range(NT):
                yield from attention(
                    tt, T,
                    lambda h: qT[(h // 4) * DH:(h // 4 + 1) * DH, h % 4, tt * P:(tt + 1) * P],
                    lambda h: kaT[(h // 4) * DH:(h // 4 + 1) * DH, :],
                    lambda kt, h: va[:, kt, (h // 4) * DH:(h // 4 + 1) * DH],
                    bias_of(bias_a, tt), ((s_t5b, 16),), buf, o_sb[:, tt, :],
                    (got["qa"], got["ka"], va_mark), SAME_GROUP, sink[:, :])
                yield
                while "u_read" not in got:
                    yield
                yield from mixed(tt, o_sb, 0, slice(0, W))
            for tt in range(NT):
                yield from attention(
                    tt, T,
                    lambda h: qbT[(h % 2) * DH:(h % 2 + 1) * DH, h // 2, tt * P:(tt + 1) * P],
                    lambda h: kT[(h % 2) * DH:(h % 2 + 1) * DH, h // 2, :],
                    lambda kt, h: v_sb[:, kt, h * DH:(h + 1) * DH],
                    bias_of(bias_b, tt), (nb_mark,), buf, ob_sb[:, tt, :],
                    (got["qb"], got["kb"], got["vb"]), SAME_PARITY)
                yield
                yield from mixed(tt, ob_sb, KW, slice(W, 2 * W))

        VE.wait((s_sink, 16))
        weave(main2(), side2())
        PE.wait(*got["mix"])
        acc = acc_banks()
        for k in range(KD):
            m = piece_a(acc, U, (k,), D, k == 0, k == KD - 1)
        last = m
        for tt in range(NT):
            for n in range(2):
                cols = slice(n * 512, (n + 1) * 512)
                b = 2 * tt + n
                m = VE.go((last, got["ada", 5]), V.tensor_tensor, xn[:, tt, cols], bank[b][:, :],
                          ada[:, 2, cols], ALU.mult)
                free[b] = (m,)
                m = VE.go((m,), V.tensor_tensor, x[:, tt, cols], x[:, tt, cols], xn[:, tt, cols], ALU.add)
        AC.wait(m, got["ada", 5])
        S.dma_start(x_dram.rearrange("t p d -> p t d"), x[:, :, :]).then_inc(s_park, 16)
        S.dma_start(gate_dram, ada[0:1, 5, :]).then_inc(s_park, 16)
        m = VE.go((m,), V.scalar_tensor_tensor, ada[:, 4, :], ada[:, 4, :], 1.0, gains_b[:, 2, :],
                  ALU.add, ALU.mult)
        norm_to_u(x, xn, ada[:, 4, :], (m,), (), ada[:, 3, :])
        ph1.close()
        Z = sb(ctx, "Z", [P, PK * T])
        sel = sb(ctx, "sel", [P, 3, T])
        rows_a, rows_b = sb(ctx, "rows_a", [P, 4, P]), sb(ctx, "rows_b", [P, 4, P])
        dist = sb(ctx, "dist", [P, 4, P])
        qhT = Z[:, 0:N_QUERY * T].rearrange("p (f t) -> p f t", t=T)
        skT = Z[:, N_QUERY * T:N_QUERY * (T + PK)].rearrange("p (f n) -> p f n", n=PK)
        at_tail = [PH * SEL_PIECES * T]

        def tail(n):
            at_tail[0] += n
            assert at_tail[0] <= PK * T
            return Z[:, at_tail[0] - n:at_tail[0]]
        scores = tail(PH * 4 * PK).rearrange("p (h n) -> p h n", h=PH)
        hs, hs2, cand, cand2, eq = tail(512), tail(512), tail(512), tail(512), tail(512)
        val = tail(64).rearrange("p (a n) -> p a n", a=4)
        idx = tail(64).rearrange("p (a n) -> p a n", a=4)
        idxf = tail(64).rearrange("p (t s n) -> p t s n", t=2, s=2)
        pick = tail(64).rearrange("p (a n) -> p a n", a=2)
        pick_hl, pick_f = tail(64), tail(64)
        best = tail(NT * P).rearrange("p (t n) -> p t n", t=NT)
        rowcol = tail(2 * NT * P).rearrange("p (s t n) -> p s t n", s=2, t=NT)
        smx = tail(2 * NT * PH).rearrange("p (a n) -> p a n", a=2)

        AC.wait((s_park, 32))
        VE.wait((s_park, 32))
        for f in range(0, N_QUERY, 2):
            b = 4 + (f // 2) % 2
            take(b)
            piece_b([bank[b][:, 0:T]], *U)
            m = piece_b([bank[b][:, T:2 * T]], *U)
            m = AC.go((m,), S.activation, qhT[:, f:f + 2, :].rearrange("p a n -> p (a n)"),
                      bank[b][:, :], ACT.Copy)
            free[b] = (m,)
            if f == 0:
                S.dma_start(skT, sub_keys).then_inc(s_sk, 16)
        PE.wait(m, (s_sk, 16))
        for h in range(PH):
            b = h % 4
            take(b)
            for tt in range(NT):
                for side in range(2):
                    i = M.matmul(bank[b][:, (2 * tt + side) * PK:(2 * tt + side + 1) * PK],
                                 qhT[:, 2 * h + side, tt * P:(tt + 1) * P], skT[:, 2 * h + side, :],
                                 start=True, stop=True, skip_group_check=True)
            t = PE.done(i)
            m = VE.go((t,), V.tensor_copy, scores[:, h, :], bank[b][:, :])
            free[b] = (m,)
        take(0), take(1), take(2), take(3), take(4), take(5)
        VE.wait(m)
        CH = Line(nc.vector, s_chain)
        S.sem_inc(s_z, 2)
        V.sem_inc(s_m, 2)
        M.sem_inc(s_g, 1)
        S.sem_inc(s_hb, 1)

        def expert_up(q, tile):
            nc.tensor.wait_ge(s_z, tile + 1)
            m = piece_b([bank[4 + q][:, 0:T]], *U)
            nc.scalar.wait_ge(*m)
            nc.scalar.activation(Z[:, bass.ds(tile * T, T)], bank[4 + q][:, 0:T],
                                 ACT.Gelu_apprx_tanh).then_inc(s_z, 1)

        def top16(src, spare, v, ix, m):
            m = CH.go((m,), V.max, v[:, 0:8], src)
            CH.go((m,), V.max_index, ix[:, 0:8], v[:, 0:8], src)
            yield
            m = CH.go((), V.match_replace, spare, v[:, 0:8], src, TAKEN)
            m = CH.go((m,), V.max, v[:, 8:16], spare)
            m = CH.go((m,), V.max_index, ix[:, 8:16], v[:, 8:16], spare)
            got["chain"] = m
            yield

        def select(h):
            m = CH.go((), V.tensor_copy, hs, scores[:, bass.ds(h, 1), :].rearrange("p a n -> p (a n)"))
            for a in range(4):
                c = slice(a * PK, (a + 1) * PK)
                yield from top16(hs[:, c], hs2[:, c], val[:, a, :], idx[:, a, :].bitcast(U32), m)
            m = got["chain"]
            m = CH.go((m,), V.tensor_copy, idxf.rearrange("p t s n -> p (t s n)"),
                      idx.rearrange("p a n -> p (a n)").bitcast(U32))
            v4 = val.rearrange("p (t s) n -> p t s n", s=2)
            for tt in range(NT):
                m = CH.go((m,), V.tensor_tensor,
                          cand[:, tt * 256:(tt + 1) * 256].rearrange("p (i j) -> p i j", j=PT),
                          v4[:, tt, 0, :].unsqueeze(2).to_broadcast([P, PT, PT]),
                          v4[:, tt, 1, :].unsqueeze(1).to_broadcast([P, PT, PT]), ALU.add)
            yield
            for tt in range(NT):
                c = slice(tt * 256, (tt + 1) * 256)
                yield from top16(cand[:, c], cand2[:, c], pick[:, 0, tt * PT:(tt + 1) * PT],
                                 pick[:, 1, tt * PT:(tt + 1) * PT].bitcast(U32), m)
            m = CH.go((got["chain"],), V.tensor_copy,
                      best[:, :, bass.ds(h * PT, PT)],
                      pick[:, 0, :].rearrange("p (t n) -> p t n", t=NT))
            places = pick[:, 1, :].bitcast(U32)
            m = CH.go((m,), V.tensor_scalar, pick_hl[:, 0:32].bitcast(U32), places, 4, None,
                      ALU.logical_shift_right)
            m = CH.go((m,), V.tensor_scalar, pick_hl[:, 32:64].bitcast(U32), places, 15, None,
                      ALU.bitwise_and)
            m = CH.go((m,), V.tensor_copy, pick_f, pick_hl.bitcast(U32))
            yield
            for side in range(2):
                e4 = eq.rearrange("p (t k m) -> p t k m", t=NT, k=PT)
                for tt in range(NT):
                    e3 = e4[:, tt, :, :]
                    pf = pick_f[:, 32 * side + PT * tt:32 * side + PT * (tt + 1)]
                    m = CH.go((m,), V.tensor_tensor, e3, pf.unsqueeze(2).to_broadcast([P, PT, PT]),
                              iota16.unsqueeze(1).to_broadcast([P, PT, PT]), ALU.is_equal)
                    m = CH.go((m,), V.tensor_tensor, e3, e3,
                              idxf[:, tt, side, :].unsqueeze(1).to_broadcast([P, PT, PT]), ALU.mult)
                m = CH.go((m,), V.tensor_reduce, rowcol[:, side, :, bass.ds(h * PT, PT)], e4,
                          AX.X, ALU.add)
                yield

        quads0, piece0 = at["quads"], at["piece"]
        with nc.Fori(0, PH, engines=compute) as h:
            at["quads"], at["piece"] = quads0 + h * (SEL_PIECES // RING), piece0
            CH.restart()

            def ups():
                for j in range(SEL_PIECES):
                    expert_up(j % 2, h * SEL_PIECES + j)
                    yield
            weave(ups(), select(h), 2)
            nc.vector.wait_ge(s_chain, CH.n)
            nc.vector.sem_clear(s_chain)
        at["quads"], at["piece"] = quads0, piece0 + PH * SEL_PIECES
        n0 = PH * SEL_PIECES

        def weigh():
            b4 = best.rearrange("p t (h k) -> p (t h) k", k=PT)
            m = VE.go((), V.tensor_tensor, cand[:, 0:NT * P].rearrange("p (g k) -> p g k", k=PT), b4,
                      b4[:, :, 0:1].to_broadcast([P, NT * PH, PT]), ALU.subtract)
            m = AC.go((m,), S.activation, best.rearrange("p t n -> p (t n)"), cand[:, 0:NT * P], ACT.Exp)
            yield
            m = VE.go((m,), V.tensor_reduce, smx[:, 0, :], b4, AX.X, ALU.add)
            m = VE.go((m,), V.reciprocal, smx[:, 1, :], smx[:, 0, :])
            m = VE.go((m,), V.tensor_tensor, b4, b4, smx[:, 1, :].unsqueeze(2).to_broadcast(
                [P, NT * PH, PT]), ALU.mult)
            yield
            PE.wait(m)
            for a, src in enumerate((best, rowcol[:, 0, :, :], rowcol[:, 1, :, :])):
                for tt in range(NT):
                    i = M.transpose(bank[a][:, tt * P:(tt + 1) * P], src[:, tt, :], ident)
            t = PE.done(i)
            yield
            for a in range(3):
                m = VE.go((t,), V.tensor_copy, sel[:, a, :], bank[a][:, 0:T])
            got["sel"] = m
            yield

        def ups2():
            for j in range(2 * RING):
                expert_up(j % 2, n0 + j)
                yield
        scores_read = VE.done(V.memset(rows_a[:, 0, 0:1], 0.0))
        AC.wait(scores_read)
        weave(ups2(), weigh())
        AC.wait(got["sel"])
        n0 += 2 * RING
        quads, piece = at["quads"], at["piece"]
        with nc.Fori(0, (PK - n0) // RING, engines=compute) as i:
            at["quads"], at["piece"] = quads + i, piece
            for j in range(RING):
                expert_up(j % 2, i * RING + (n0 + j))
        at["quads"], at["piece"] = quads, piece + PK - n0

        byt = Z[:, :].rearrange("p (j t) -> p t j", t=T)
        G.wait_ge(*got["sel"])
        M.wait_ge(*got["sel"])
        V.wait_ge(s_z, PK + 2)
        M.wait_ge(s_z, PK + 2)
        with nc.Fori(0, T // 8, engines=compute) as i:
            for q in range(2):
                turn_no = i * 2 + q
                t0 = i * 8 + 4 * q
                ra, rb = rows_a, rows_b
                G.wait_ge(s_hb, turn_no + 1)
                G.tensor_tensor(dist[:, :, :], iota.unsqueeze(1).to_broadcast([P, 4, P]),
                                sel[:, 2, bass.ds(t0, 4)].unsqueeze(2).to_broadcast([P, 4, P]),
                                ALU.subtract).then_inc(s_d, 1)
                G.wait_ge(s_d, turn_no * 2 + 1)
                G.tensor_tensor(dist[:, :, :], dist[:, :, :], dist[:, :, :], ALU.mult).then_inc(s_d, 1)
                S.wait_ge(s_d, turn_no * 2 + 2)
                S.wait_ge(s_g, turn_no + 1)
                S.activation(rb[:, :, :], dist[:, :, :], ACT.Relu, bias=1.0, scale=-1.0).then_inc(s_hb, 1)
                V.wait_ge(s_g, turn_no + 1)
                for e in range(4):
                    ins = V.tensor_scalar(ra[:, e, :], iota, sel[:, 1, bass.ds(t0 + e, 1)],
                                          sel[:, 0, bass.ds(t0 + e, 1)], ALU.is_equal, ALU.mult)
                ins.then_inc(s_ha, 1)
                M.wait_ge(s_ha, turn_no + 1)
                M.wait_ge(s_hb, turn_no + 2)
                M.wait_ge(s_m, turn_no + 1)
                for e in range(4):
                    ins = M.matmul(bank[q][:, e * P:(e + 1) * P], ra[:, e, :], rb[:, e, :],
                                   start=True, stop=True, skip_group_check=True)
                ins.then_inc(s_g, 1)
                V.wait_ge(s_g, turn_no + 2)
                zt = byt[:, bass.ds(t0, 4), :]
                V.tensor_tensor(zt, zt, bank[q][:, :].rearrange("p (t j) -> p t j", t=4),
                                ALU.mult).then_inc(s_m, 1)

        S.wait_ge(s_m, T // 4 + 2)
        V.wait_ge(s_m, T // 4 + 2)
        M.wait_ge(s_m, T // 4 + 2)

        def expert_down(q, tile, first, last, drained):
            zj = Z[:, bass.ds(tile * T, T)]
            read = dyn(RING) + (at["piece"] - 1)
            if not first:
                S.wait_ge(s_used, read)
            S.activation(a_hi[:, q, :], zj, ACT.Copy).then_inc(s_ah, 1)
            V.wait_ge(s_ah, tile + 1)
            V.tensor_tensor(a_lo[:, q, :], zj, a_hi[:, q, :].bitcast(F32), ALU.subtract).then_inc(s_al, 1)
            s = next_piece(drained)
            M.wait_ge(s_al, tile + 1)
            for tt in range(NT):
                for n in range(2):
                    ins = mm3(acc[tt][n], a_hi[:, q, tt * P:(tt + 1) * P],
                              a_lo[:, q, tt * P:(tt + 1) * P], w_hi[:, s, n * 512:(n + 1) * 512],
                              w_lo[:, s, n * 512:(n + 1) * 512], first, last)
            return used(ins)

        acc = [[bank[0][:, :], bank[1][:, :]], [bank[2][:, :], bank[3][:, :]]]
        for j in range(RING):
            expert_down(j % 2, j, j == 0, False, False)
        quads, piece = at["quads"], at["piece"]
        with nc.Fori(0, PK // RING - 2, engines=compute) as i:
            at["quads"], at["piece"] = quads + i, piece
            for j in range(RING):
                expert_down(j % 2, i * RING + (RING + j), False, False, False)
        at["quads"], at["piece"] = quads, piece + PK - 2 * RING
        S.wait_ge(s_used, N_PIECES - PK // 2)
        S.wait_ge(s_al, PK // 2)
        xr = Z[:, 0:NT * D].rearrange("p (t n) -> p t n", t=NT)
        g2, gf = Z[:, NT * D:(NT + 1) * D], Z[:, (NT + 1) * D:(NT + 2) * D]
        yo = Z[:, (NT + 2) * D:(2 * NT + 2) * D].rearrange("p (t n) -> p t n", t=NT)
        S.dma_start(xr, x_dram.rearrange("t p d -> p t d")).then_inc(s_back, 16)
        S.dma_start(g2, gate_dram.partition_broadcast(P).rearrange("p a n -> p (a n)")).then_inc(s_back, 16)
        S.dma_start(gf, gain_out.partition_broadcast(P).rearrange("p a n -> p (a n)")).then_inc(s_back, 16)
        for j in range(RING):
            n = PK - RING + j
            m = expert_down(j % 2, n, False, j == RING - 1, at["piece"] + AHEAD >= N_PIECES)
        assert at["piece"] == N_PIECES, (at["piece"], N_PIECES)
        VE.wait((s_back, 48))
        S.wait_ge(s_back, 48)
        for tt in range(NT):
            for n in range(2):
                cols = slice(n * 512, (n + 1) * 512)
                mm_ = VE.go((m,), V.tensor_tensor, yo[:, tt, cols], bank[2 * tt + n][:, :], g2[:, cols],
                            ALU.mult)
                mm_ = VE.go((mm_,), V.tensor_tensor, xr[:, tt, cols], xr[:, tt, cols], yo[:, tt, cols],
                            ALU.add)
            r, _, mr = row_scale(tt, xr[:, tt, :], D, 0, yo[:, tt, :], (mm_,))
            mr = VE.go((mr,), V.scalar_tensor_tensor, yo[:, tt, :], xr[:, tt, :], r, gf, ALU.mult, ALU.mult)
            nc.sync.wait_ge(*mr)
            nc.sync.dma_start(out[tt * P:(tt + 1) * P, :], yo[:, tt, :]).then_inc(s_out, 16)
        nc.sync.wait_ge(s_out, 16 * NT)


def pieces_b(w):
    k, f = w.shape[0] // P, w.shape[1] // P
    return w.reshape(k, P, f, P).transpose(2, 1, 0, 3).reshape(f, P, k * P)


def pieces_b4(w):
    return w.reshape(KW, P, KD // 2, 2, P).transpose(2, 1, 3, 0, 4).reshape(KD // 2, P, PIECE)


def pieces_a(w):
    return w.reshape(-1, P, w.shape[1])


def pieces_v(w):
    return w.reshape(KD // 2, 2, P, W).transpose(0, 2, 1, 3).reshape(KD // 2, P, PIECE)


def interleaved(up, down):
    order = [up[0], up[1]]
    for j in range(KH - 2):
        order += [up[j + 2], down[j]]
    return np.stack(order + [down[KH - 2], down[KH - 1]])


def weight_stream(a):
    parts = []
    cuts = np.cumsum([W, W, W, IH * DH, DH, IH, W, W, W, 2 * D])
    for l in range(LAYERS):
        q, k, v, iq, ik, iw, cb, cc, ch, g = np.split(a["w_in"][l], cuts[:-1], axis=1)
        parts += [pieces_b(np.concatenate([iw, np.zeros((D, P - IH), np.float32)], 1)), pieces_b(iq),
                  pieces_b(np.concatenate([ik, ik], 1)), pieces_b(k), pieces_b(q), pieces_v(v)]
        cc, ch = pieces_b(cc), pieces_b(ch)
        parts += [cc[0:2], ch[0:2], cc[2:4], ch[2:4], pieces_b(cb), pieces_b(g)]
        pair = np.stack([pieces_b4(a["w_attn_out"][l]), pieces_b4(a["w_conv_out"][l])], 1)
        parts += [pair.reshape(-1, P, PIECE), pieces_a(a["w_mix_out"][l]),
                  interleaved(pieces_b(a["w_mlp_up"][l]), pieces_a(a["w_mlp_down"][l]))]
    ada = a["w_ada_2"][0].reshape(KD, P, 6, D).transpose(2, 0, 1, 3)
    qa, ka, va, qb, kb, vb = np.split(a["w_in_2"][0], np.cumsum([W, P, P, W, W]), axis=1)
    qa = qa.reshape(D, 2, KW, DH).transpose(0, 2, 1, 3).reshape(D, W)
    parts += [ada[0:2].reshape(-1, P, D), pieces_b(ka), pieces_b(qa), pieces_b(va), pieces_b(kb), pieces_b(qb),
              pieces_v(vb), ada[2:6].reshape(-1, P, D), pieces_a(a["w_out_2"][0]),
              pieces_b(a["w_query_2"][0])]
    u = a["u_experts_2"][0].reshape(PK, PK, KD, P).transpose(1, 3, 2, 0).reshape(PK, P, PIECE)
    v = a["v_experts_2"][0].reshape(PK, P, D).transpose(1, 0, 2)
    return np.concatenate(parts + [u, v])


def kept_table():
    row = np.arange(P, dtype=np.float32)
    return np.concatenate([np.eye(P, dtype=np.float32), np.tile(row, (P, 1)),
                           np.tile(row[:PT], (P, 1))], 1)


def rope_table():
    half = ROPE // 2
    inv = (1.0 / (np.float32(ROPE_THETA) ** (np.arange(0, ROPE, 2, dtype=np.float32) / ROPE))
           ).astype(np.float32)
    ang = np.arange(T, dtype=np.float32)[:, None] * inv[None, :]
    cos, sin = np.ones((P, T), np.float32), np.zeros((P, T), np.float32)
    turn = np.zeros((P, P), np.float32)
    for f in range(P):
        d = f % DH
        if d < ROPE:
            cos[f] = np.cos(ang[:, d % half])
            sin[f] = np.sin(ang[:, d % half]) * (-1.0 if d < half else 1.0)
            turn[f + half if d < half else f - half, f] = 1.0
    return np.concatenate([cos, cos, sin, sin, turn], 1)


def t5_table_of_distance():
    rel = np.arange(T5_W) - (T - 1)
    half, exact = T5_BUCKETS // 2, T5_BUCKETS // 4
    n = np.abs(rel)
    nf = np.maximum(n, 1).astype(np.float32)
    large = exact + (np.log(nf / np.float32(exact)) / np.float32(np.log(T5_MAX / exact))
                     * (half - exact)).astype(np.int32)
    bucket = np.where(rel > 0, half, 0) + np.where(n < exact, n, np.minimum(large, half - 1))
    hot = np.zeros((DH, T5_W), np.float32)
    inside = n <= WINDOW
    hot[bucket[inside], np.arange(T5_W)[inside]] = 1.0
    hot[T5_BUCKETS, ~inside] = -BIG
    return hot


def na_column_mask():
    c = np.arange(GRID_W)
    start = np.clip(c - NA_COLS // 2, 0, GRID_W - NA_COLS)
    seen = (c[None, :] >= start[:, None]) & (c[None, :] < start[:, None] + NA_COLS)
    return np.tile(np.where(seen, 0.0, -BIG).astype(np.float32), (2, 1))


def kernel(**inputs):
    import concourse.bacc as bacc
    from concourse.bass_utils import run_bass_kernel_spmd

    a = {k: np.asarray(v) for k, v in inputs.items()}
    t5 = np.zeros((DH, H), np.float32)
    t5[0:T5_BUCKETS], t5[T5_BUCKETS] = a["t5_table_2"], 1.0
    rpb = np.zeros((H, 2 * NA_ROWS - 1, P), np.float32)
    rpb[:, :, GRID_W - NA_COLS:GRID_W + NA_COLS - 1] = a["rpb_b_2"][0]
    arrays = {
        "stream": weight_stream(a),
        "x_in": a["x"][0],
        "gains1": np.concatenate([a["norm_mix"], a["norm_mlp"]]),
        "gains2": np.concatenate([a["norm_final"][None], a["norm1_g_2"], a["norm2_g_2"],
                                  np.concatenate([a["out_norm_a_2"], a["out_norm_b_2"]], 1)]),
        "conv_w": a["conv_w"].reshape(LAYERS, TAPS, KW, P).transpose(3, 0, 2, 1).reshape(
            P, LAYERS, KW * TAPS),
        "b_ada": a["b_ada_2"][0].reshape(6, D),
        "c_cols": a["c_2"][0].reshape(KD, P).T,
        "kept_in": kept_table(),
        "rope_in": rope_table(),
        "na_mask_in": na_column_mask(),
        "t5_in": t5,
        "t5_hot": t5_table_of_distance(),
        "rpb_pad": rpb[:, NA_ROWS - ROWS:NA_ROWS - ROWS + NA_DR].reshape(1, -1),
        "sinks": a["sink_a_2"][0],
        "sub_keys": a["sub_keys_2"][0].transpose(3, 0, 1, 2).reshape(P, N_QUERY, PK),
        "gain_out": a["final_g_2"].reshape(1, D),
    }
    arrays = {k: np.ascontiguousarray(v) for k, v in arrays.items()}
    nc = bacc.Bacc("TRN2", target_bir_lowering=False, num_devices=1)
    args = {k: nc.dram_tensor(k, v.shape, F32, kind="ExternalInput").ap() for k, v in arrays.items()}
    out = nc.dram_tensor("out", (T, D), F32, kind="ExternalOutput").ap()
    build(nc, out=out, **args)
    r = run_bass_kernel_spmd(nc, [arrays], core_ids=[0])
    return r.results[0]["out"].reshape(1, T, D)
```

```python
import numpy as np
from contextlib import ExitStack

import concourse.bass as bass
from concourse import mybir

F32 = mybir.dt.float32
F32R = mybir.dt.float32r
U32 = mybir.dt.uint32
ALU = mybir.AluOpType
ACT = mybir.ActivationFunctionType
AX = mybir.AxisListType
ENG = mybir.EngineType

P = 128
T, D = 256, 1024
NT, KD = T // P, D // P
LAYERS = 2
H, DH = 8, 64
W = H * DH
KW = W // P
IH = 4
TOPK = T // 4
CHUNK = 64
TAPS = 3
HID = 4 * D
KH = HID // P
ROPE, ROPE_THETA = DH // 4, 500000.0
EPS = 1e-6
WINDOW, T5_BUCKETS, T5_MAX = 128, 32, 128
GRID_W, NA_ROWS, NA_COLS = 64, 8, 16
ROWS = T // GRID_W
PH, PK, PT = 8, 128, 16
BIAS_W = T + P
T5_W = BIAS_W + P
NA_DR = 2 * ROWS - 1
BIG = 1e30
OUT_OF_BLOCK = -3.0e38
TAKEN = -3.4e38

PIECE = 1024
RING = 4
AHEAD = 3
N_LAYER = 60 + 2 * KH
N_ADA = 6 * KD
N_MIXER2 = 18 + KD
N_QUERY = 2 * PH
N_PIECES = LAYERS * N_LAYER + N_ADA + N_MIXER2 + N_QUERY + 2 * PK
SEL_PIECES = 8
FIRST = PH * SEL_PIECES + RING
assert N_LAYER % RING == 0 and N_ADA % RING == 0


class Line:

    def __init__(self, eng, sem):
        self.eng, self.sem, self.n, self.seen = eng, sem, 0, {}

    def wait(self, *marks):
        for mark in marks:
            if mark is None:
                continue
            sem, value = mark
            if isinstance(value, int):
                if self.seen.get(sem.name, 0) >= value:
                    continue
                self.seen[sem.name] = value
            self.eng.wait_ge(sem, value)

    def done(self, instruction):
        instruction.then_inc(self.sem, 1)
        self.n += 1
        return self.sem, self.n

    def go(self, marks, method, *args, **kw):
        self.wait(*marks)
        return self.done(method(*args, **kw))

    def restart(self):
        self.n, self.seen = 0, {}


def build(nc, stream, x_in, gains1, gains2, conv_w, b_ada, c_cols, kept_in, rope_in, na_mask_in,
          t5_in, t5_hot, rpb_pad, sinks, sub_keys, gain_out, out):
    ctx = ExitStack()
    with ctx:
        def sb(c, name, shape, dt=F32):
            return c.enter_context(nc.sbuf_tensor(name, shape, dt))

        def sem(name):
            return ctx.enter_context(nc.semaphore(name))

        t5_dram = nc.dram_tensor("t5_by_distance", [1, H * T5_W], F32, kind="Internal").ap()
        t5_rows = nc.dram_tensor("t5_rows", [P, H * T5_W], F32, kind="Internal").ap()
        rpb_rows = nc.dram_tensor("rpb_rows", [GRID_W, H * NA_DR * P], F32, kind="Internal").ap()
        x_dram = nc.dram_tensor("x_parked", [NT, P, D], F32, kind="Internal").ap()
        gate_dram = nc.dram_tensor("gate2_parked", [1, D], F32, kind="Internal").ap()

        raw = sb(ctx, "raw", [P, RING, PIECE])
        w_hi = sb(ctx, "w_hi", [P, RING, PIECE], F32R)
        w_lo = sb(ctx, "w_lo", [P, RING, PIECE], F32R)
        u_hi = sb(ctx, "u_hi", [P, KD, T], F32R)
        u_lo = sb(ctx, "u_lo", [P, KD, T], F32R)
        a_hi = sb(ctx, "a_hi", [P, 2, T], F32R)
        a_lo = sb(ctx, "a_lo", [P, 2, T], F32R)
        kept = sb(ctx, "kept", [P, 2 * P + PT])
        ident, iota, iota16 = kept[:, 0:P], kept[:, P:2 * P], kept[:, 2 * P:2 * P + PT]
        st = sb(ctx, "st", [P, 10, NT])
        c_col, c_tmp = sb(ctx, "c_col", [P, KD]), sb(ctx, "c_tmp", [P, 2, KD])
        c_hi, c_lo = sb(ctx, "c_hi", [P, KD], F32R), sb(ctx, "c_lo", [P, KD], F32R)
        c_col = c_col[:, :]
        bank = [ctx.enter_context(nc.psum_tensor(f"bank{i}", [P, 512], F32)) for i in range(8)]

        landed = [sem(f"landed{i}") for i in range(RING)]
        s_hi = sem("s_hi")
        s_split = sem("s_split")
        s_used = sem("s_used")
        s_relu = sem("s_relu")
        s_act = sem("s_act")
        s_kept, s_gain0, s_gain, s_cw, s_rope, s_c = (sem(n) for n in (
            "s_kept", "s_gain0", "s_gain", "s_cw", "s_rope", "s_c"))
        s_t5, s_t5w, s_t5b, s_na, s_gain2, s_bada, s_sink, s_naw, s_sk = (sem(n) for n in (
            "s_t5", "s_t5w", "s_t5b", "s_na", "s_gain2", "s_bada", "s_sink", "s_naw", "s_sk"))
        s_x = [sem(f"s_x{i}") for i in range(2 * NT)]
        s_t5c = sem("s_t5c")
        s_park, s_back, s_out = sem("s_park"), sem("s_back"), sem("s_out")
        s_d = sem("s_d")
        s_z, s_chain, s_ha, s_hb, s_g, s_m, s_ah, s_al = (sem(n) for n in (
            "s_z", "s_chain", "s_ha", "s_hb", "s_g", "s_m", "s_ah", "s_al"))
        PE = Line(nc.tensor, sem("s_pe"))
        AC = Line(nc.scalar, sem("s_ac"))
        VE = Line(nc.vector, sem("s_ve"))
        lines = (PE, AC, VE)
        compute = bass.OrderedEngineSet([ENG.PE, ENG.Activation, ENG.DVE])
        V, S, M, G = nc.vector, nc.scalar, nc.tensor, nc.gpsimd

        nc.sync.dma_start(kept[:, :], kept_in).then_inc(s_kept, 16)
        for s in range(RING):
            nc.sync.dma_start(raw[:, s, :], stream[s]).then_inc(landed[s], 16)
        def load_piece(i, s):
            nc.sync.wait_ge(s_split, i * RING + (s + 1 - RING))
            nc.sync.dma_start(raw[:, s, :], stream[bass.ds(i * RING + s, 1), :, :].rearrange(
                "a p n -> (a p) n")).then_inc(landed[s], 16)
        with nc.sync.Fori(1, N_PIECES // RING) as i:
            for s in range(RING):
                load_piece(i, s)
        for s in range(N_PIECES % RING):
            load_piece(N_PIECES // RING, s)

        at = {"piece": 0, "quads": 0}

        def dyn(k):
            return at["quads"] * k

        def split(c):
            s = c % RING
            nc.scalar.wait_ge(landed[s], dyn(16) + 16 * (c // RING + 1))
            if c >= RING:
                nc.scalar.wait_ge(s_used, dyn(RING) + (c - RING + 1))
            nc.scalar.activation(w_hi[:, s, :], raw[:, s, :], ACT.Copy).then_inc(s_hi, 1)
            nc.vector.wait_ge(s_hi, dyn(RING) + (c + 1))
            nc.vector.tensor_tensor(w_lo[:, s, :], raw[:, s, :], w_hi[:, s, :].bitcast(F32),
                                    ALU.subtract).then_inc(s_split, 1)

        def next_piece(last=False):
            c = at["piece"]
            at["piece"] = c + 1
            if not last:
                split(c + AHEAD)
            nc.tensor.wait_ge(s_split, dyn(RING) + (c + 1))
            return c % RING

        def used(instruction):
            instruction.then_inc(s_used, 1)
            return s_used, dyn(RING) + at["piece"]

        def mm3(o, lh, ll, rh, rl, start, stop):
            M.matmul(o, lh, rh, start=start, stop=False, skip_group_check=True)
            M.matmul(o, lh, rl, start=False, stop=False, skip_group_check=True)
            return M.matmul(o, ll, rh, start=False, stop=stop, skip_group_check=True)

        def piece_b(o, rhs_hi, rhs_lo, kt=KD, parts=1, last=False):
            s = next_piece(last)
            for part in range(parts):
                for k in range(kt):
                    col = (part * kt + k) * P
                    i = mm3(o[part], w_hi[:, s, col:col + P], w_lo[:, s, col:col + P],
                            rhs_hi[:, k, :], rhs_lo[:, k, :], k == 0, k == kt - 1)
            return used(i)

        def piece_a(o, lhs, ks, width, first, final):
            s = next_piece()
            for j, k in enumerate(ks):
                for tt in range(NT):
                    lh, ll = (u[:, k, tt * P:(tt + 1) * P] for u in lhs)
                    for n in range(width // 512):
                        col = j * width + n * 512
                        i = mm3(o[tt][n], lh, ll, w_hi[:, s, col:col + 512],
                                w_lo[:, s, col:col + 512], first and j == 0,
                                final and j == len(ks) - 1)
            return used(i)

        def run(steps):
            for _ in steps:
                pass

        ss_marks, norm_late, scales = [], [], []
        free = {}

        def take(i):
            PE.wait(*free.get(i, ()))

        def restart_lines():
            nc.multi_engine_barrier(compute)
            for line in lines:
                line.eng.sem_clear(line.sem)
                line.restart()
            nc.multi_engine_barrier(compute)
            free.clear()
            scales[:] = [None]

        def transposes(b, sources, marks):
            take(b)
            PE.wait(*marks)
            for j, src in enumerate(sources):
                i = M.transpose(bank[b][:, j * P:(j + 1) * P], src, ident)
            return PE.done(i)

        def split_bank(src, hi, lo, mark, extra=()):
            m = AC.go((mark, *extra), S.activation, hi, src, ACT.Copy)
            return VE.go((m, mark), V.tensor_tensor, lo, src, hi.bitcast(F32), ALU.subtract), m

        def inverse_root(ss, width, n):
            c = [ss[:, j, 0:n] for j in range(5)]
            m = VE.go(ss_marks, V.tensor_scalar, c[1], c[0], 1.0 / width, EPS, ALU.mult, ALU.add)
            m = VE.go((m,), V.reciprocal, c[2], c[1])
            m = AC.go((m,), S.activation, c[3], c[2], ACT.Sqrt)
            m = VE.go((m,), V.tensor_tensor, c[4], c[3], c[3], ALU.mult)
            m = VE.go((m,), V.tensor_tensor, c[4], c[4], c[1], ALU.mult)
            m = VE.go((m,), V.tensor_scalar, c[4], c[4], -0.5, 1.5, ALU.mult, ALU.add)
            return VE.go((m,), V.tensor_tensor, c[3], c[4], c[3], ALU.mult)

        def row_scales(x, junk, marks):
            for tt in range(NT):
                for n in range(2):
                    cols = slice(n * 512, (n + 1) * 512)
                    m = AC.go((marks[tt][n],), S.activation, junk[:, tt, cols], x[:, tt, cols],
                              ACT.Square, accum_out=st[:, 5 + n, tt:tt + 1])
                yield
            m = VE.go((m,), V.tensor_tensor, st[:, 0, :], st[:, 5, :], st[:, 6, :], ALU.add)
            ss_marks[:] = [m]
            scales[:] = [inverse_root(st, D, NT)]
            yield

        def norm_to_u(x, xn, gain, marks, shift=None):
            yield from row_scales(x, xn, marks)
            yield from scaled_to_u(x, xn, gain, shift)

        def scaled_to_u(x, xn, gain, shift=None):
            r = scales[0]
            for tt in range(NT):
                for g in range(KD // 4):
                    cols = slice(g * 512, (g + 1) * 512)
                    m = VE.go((r,), V.scalar_tensor_tensor, xn[:, tt, cols], x[:, tt, cols],
                              st[:, 3, tt:tt + 1], gain[:, cols], ALU.mult, ALU.mult)
                    if shift is not None:
                        m = VE.go((m,), V.tensor_tensor, xn[:, tt, cols], xn[:, tt, cols],
                                  shift[:, cols], ALU.add)
                    b = (6, 7, 0, 1)[2 * tt + g]
                    t = transposes(b, [xn[:, tt, k * P:(k + 1) * P] for k in range(4 * g, 4 * g + 4)],
                                   (m,))
                    rows = slice(tt * P, (tt + 1) * P)
                    m1 = AC.go((t,), S.activation, u_hi[:, 4 * g:4 * g + 4, rows],
                               bank[b][:, :].rearrange("p (k n) -> p k n", k=4), ACT.Copy)
                    pending = (b, g, rows, m1, t)
                    norm_late.append(pending)
                    if len(norm_late) > 2:
                        lower(*norm_late.pop(0))
                    yield
            while norm_late:
                m2 = lower(*norm_late.pop(0))
            PE.wait(m1, m2)

        def lower(b, g, rows, m1, t):
            dst = u_lo[:, 4 * g:4 * g + 4, rows]
            m = VE.go((m1, t), V.tensor_tensor, dst, bank[b][:, :].rearrange("p (k n) -> p k n", k=4),
                      u_hi[:, 4 * g:4 * g + 4, rows].bitcast(F32), ALU.subtract)
            free[b] = (m1, m)
            return m

        def add_to_x(x, mark):
            out_marks = [[None, None], [None, None]]
            AC.go((), S.activation, st[:, 9, 0:1], kept[:, 0:1], ACT.Square)
            for tt in range(NT):
                for n in range(2):
                    b = 2 * tt + n
                    cols = x[:, tt, n * 512:(n + 1) * 512]
                    m = VE.go((mark,), V.tensor_tensor, cols, cols, bank[b][:, :], ALU.add)
                    free[b] = (m,)
                    out_marks[tt][n] = m
            return out_marks

        def acc_banks():
            for b in range(4):
                take(b)
            return [[bank[0][:, :], bank[1][:, :]], [bank[2][:, :], bank[3][:, :]]]

        SAME_GROUP = [slice(h, h + 2) for h in range(0, H, 2)]
        SAME_PARITY = [slice(h, h + 3, 2) for h in (0, 1, 4, 5)]

        def attention(tt, nk, q, k, v, bias, bias_mark, buf, o, marks, pairs, sink=None):
            p, pt = buf["p"], buf["pt"]
            mx, nm, sm, ri, es = (buf["rows"][:, j, :] for j in range(5))
            for hp in range(H // 2):
                sbank = buf["score_banks"][hp]
                take(sbank)
                PE.wait(*marks)
                for e, h in enumerate(range(H)[pairs[hp]]):
                    i = M.matmul(bank[sbank][:, e * nk:(e + 1) * nk], q(h), k(h), start=True, stop=True,
                                 skip_group_check=True)
                m = PE.done(i)
                m = VE.go((m, *bias_mark, buf.get("p_free")), V.scalar_tensor_tensor,
                          p[:, pairs[hp], 0:nk],
                          bank[sbank][:, 0:2 * nk].rearrange("p (a n) -> p a n", a=2),
                          DH ** -0.5, bias(pairs[hp]), ALU.mult, ALU.add)
                free[sbank] = (m,)
                if hp % 2:
                    yield
            if sink is None:
                m = VE.go((m,), V.tensor_reduce, nm, p[:, :, 0:nk], AX.X, ALU.max, negate=True)
            else:
                m = VE.go((m,), V.tensor_reduce, mx, p[:, :, 0:nk], AX.X, ALU.max)
                m = VE.go((m,), V.tensor_tensor, mx, mx, sink, ALU.max)
                m = VE.go((m,), V.tensor_scalar, nm, mx, -1.0, None, ALU.mult)
                m = VE.go((m,), V.tensor_tensor, es, sink, nm, ALU.add)
            yield
            if sink is not None:
                e_m = AC.go((m,), S.activation, es, es, ACT.Exp)
            for h in range(H):
                m1 = AC.go((m,), S.activation, p[:, h, 0:nk], p[:, h, 0:nk], ACT.Exp,
                           bias=nm[:, h:h + 1], accum_out=sm[:, h:h + 1])
                if h % 3 == 2:
                    yield
            if sink is not None:
                m = VE.go((m1, e_m), V.tensor_tensor, sm, sm, es, ALU.add)
                m = VE.go((m,), V.reciprocal, ri, sm)
            else:
                m = VE.go((m1,), V.reciprocal, ri, sm)
            yield
            n = 0
            for kt in range(nk // P):
                for g in range(2):
                    b = buf["turn_banks"][n % 2]
                    t = transposes(b, [p[:, h, kt * P:(kt + 1) * P] for h in range(4 * g, 4 * g + 4)],
                                   (m1,))
                    dst = pt[:, kt, 4 * g:4 * g + 4, :]
                    src = bank[b][:, :].rearrange("p (h n) -> p h n", h=4)
                    if n % 2:
                        e1 = VE.go((t, buf.get("pt_free")), V.tensor_copy, dst, src)
                    else:
                        e1 = AC.go((t, buf.get("pt_free")), S.activation, dst, src, ACT.Copy)
                    free[b] = (e1,)
                    PE_marks = buf.setdefault("pt_marks", {})
                    PE_marks[n] = e1
                    n += 1
                yield
            buf["p_free"] = t
            PE.wait(*buf["pt_marks"].values())
            b = buf["turn_banks"][0]
            take(b)
            for h in range(H):
                for kt in range(nk // P):
                    i = M.matmul(bank[b][:, h * DH:(h + 1) * DH], pt[:, kt, h, :], v(kt, h),
                                 start=kt == 0, stop=kt == nk // P - 1, skip_group_check=True)
            t = PE.done(i)
            buf["pt_free"] = t
            yield
            m = VE.go((t, m), V.tensor_tensor, o.rearrange("p (h d) -> p h d", h=H),
                      bank[b][:, :].rearrange("p (h d) -> p h d", h=H),
                      ri.unsqueeze(2).to_broadcast([P, H, DH]), ALU.mult)
            free[b] = (m,)
            buf["done"] = m

        def weave(main, side, every=1):
            for n, _ in enumerate(main):
                for _ in range(every):
                    next(side, None)
            for _ in side:
                pass

        ph1 = ctx.enter_context(ExitStack())
        x = sb(ph1, "x", [P, NT, D])
        xn = sb(ph1, "xn", [P, NT, D])
        buf = {"p": sb(ph1, "p", [P, H, T]), "pt": sb(ph1, "pt", [P, NT, H, P]),
               "rows": sb(ph1, "rows", [P, 5, H]), "score_banks": (0, 1, 2, 3), "turn_banks": (6, 7)}
        o_sb = sb(ph1, "o_sb", [P, NT, W])
        qT, kT = sb(ph1, "qT", [P, KW, T]), sb(ph1, "kT", [P, KW, T])
        v_sb = sb(ph1, "v_sb", [P, NT, W])

        ph1a = ph1.enter_context(ExitStack())
        gains = sb(ph1a, "gains", [P, 2 * LAYERS, D])
        rope = sb(ph1a, "rope", [P, 2, 2 * T])
        turn = sb(ph1a, "turn", [P, P])
        cw_all = sb(ph1a, "cw_all", [P, LAYERS, KW * TAPS])
        cw = sb(ph1a, "cw", [P, KW, TAPS])
        gate = sb(ph1a, "gate", [P, 2 * KD, T])
        iqT, ikT = sb(ph1a, "iqT", [P, 2, T]), sb(ph1a, "ikT", [P, T])
        iwT, iw = sb(ph1a, "iwT", [P, T]), sb(ph1a, "iw", [P, NT, IH])
        work = sb(ph1a, "work", [P, 2, T])
        score, sbias = sb(ph1a, "score", [P, NT, T]), sb(ph1a, "sbias", [P, NT, T])
        top8 = sb(ph1a, "top8", [P, 8])
        rot = sb(ph1a, "rot", [P, 2, 2 * T])
        cc = sb(ph1a, "cc", [P, 2, 2 * T])
        prod = sb(ph1a, "prod", [P, KW, T + TAPS - 1])
        yc = sb(ph1a, "yc", [P, KW, T])
        o_hi, o_lo = sb(ph1a, "o_hi", [P, KW, T], F32R), sb(ph1a, "o_lo", [P, KW, T], F32R)
        y_hi, y_lo = sb(ph1a, "y_hi", [P, KW, T], F32R), sb(ph1a, "y_lo", [P, KW, T], F32R)
        relu = qT[:, 0:2, :]

        for tt in range(NT):
            for n in range(2):
                cols = slice(n * 512, (n + 1) * 512)
                S.dma_start(x[:, tt, cols], x_in[tt * P:(tt + 1) * P, cols]).then_inc(s_x[2 * tt + n], 16)
        S.dma_start(gains[:, 0, :], gains1[0:1, :].partition_broadcast(P).rearrange("p a n -> p (a n)")
                    ).then_inc(s_gain0, 16)
        hot = buf["p"][0:DH, 0:2, :].rearrange("p a n -> p (a n)")
        t5 = buf["p"][0:DH, 2, 0:H]
        t5_row = buf["p"][0:H, 3:5, :].rearrange("p a n -> p (a n)")
        G.dma_start(hot, t5_hot).then_inc(s_t5, 16)
        G.dma_start(t5, t5_in).then_inc(s_t5, 16)
        G.dma_start(c_col, c_cols).then_inc(s_c, 16)
        G.dma_start(rope[:, :, :].rearrange("p a n -> p (a n)"), rope_in[:, 0:4 * T]).then_inc(s_rope, 16)
        G.dma_start(turn[:, :], rope_in[:, 4 * T:4 * T + P]).then_inc(s_rope, 16)
        G.dma_start(cw_all[:, :, :], conv_w).then_inc(s_cw, 16)
        G.dma_start(gains[:, 1:, :], gains1[1:, :].partition_broadcast(P)).then_inc(s_gain, 16)
        nc.vector.memset(prod[:, :, 0:TAPS - 1], 0.0)
        t = PE.go(((s_t5, 32),), M.matmul, bank[7][0:H, :], t5, hot, start=True, stop=True)
        V.wait_ge(*t)
        V.tensor_copy(t5_row, bank[7][0:H, :]).then_inc(s_t5c, 1)
        G.dma_start(rpb_rows, rpb_pad.partition_broadcast(GRID_W).rearrange("p a n -> p (a n)")
                    ).then_inc(s_naw, 16)
        G.wait_ge(s_t5c, 1)
        G.dma_start(t5_dram.rearrange("a (h n) -> (a h) n", h=H), t5_row).then_inc(s_t5w, 16)
        G.wait_ge(s_t5w, 16)
        G.dma_start(t5_rows, t5_dram.partition_broadcast(P).rearrange("p a n -> p (a n)")).then_inc(s_t5w, 16)
        m = AC.go(((s_c, 16),), S.activation, c_tmp[:, 0, :], c_col, ACT.Sigmoid)
        m = VE.go((m, (s_c, 16)), V.tensor_tensor, c_tmp[:, 1, :], c_tmp[:, 0, :], c_col, ALU.mult)
        split_bank(c_tmp[:, 1, :], c_hi[:, :], c_lo[:, :], m)
        for c in range(AHEAD):
            split(c)

        AC.wait((s_kept, 16))
        PE.wait((s_kept, 16))
        run(row_scales(x, xn, [[(x_sem, 16) for x_sem in s_x[2 * tt:2 * tt + 2]] for tt in range(NT)]))
        VE.wait((s_gain0, 16), *[(x_sem, 16) for x_sem in s_x])
        with nc.Fori(0, LAYERS, engines=compute) as layer:
            at["quads"] = layer * (N_LAYER // RING)
            restart_lines()
            buf.pop("p_free", None), buf.pop("pt_free", None)
            run(scaled_to_u(x, xn, gains[:, bass.ds(layer * 1, 1), :].rearrange("p a n -> p (a n)")))
            cw_m = VE.go(((s_cw, 16),), V.tensor_copy, cw[:, :, :].rearrange("p a b -> p (a b)"),
                         cw_all[:, bass.ds(layer * 1, 1), :].rearrange("p a n -> p (a n)"))
            U = (u_hi, u_lo)
            got = {}

            def main_part():
                take(4)
                m = piece_b([bank[4][:, 0:T]], *U)
                got["iwT"] = AC.go((m,), S.activation, iwT[0:32, :], bank[4][0:32, 0:T], ACT.Copy)
                free[4] = (got["iwT"],)
                yield
                plan = [("iq", iqT, 0, 2), ("ik", ikT, 0, 1), ("k", kT, 0, 2), ("k", kT, 2, 2),
                        ("q", qT, 0, 2), ("q", qT, 2, 2)]
                for n, (name, dst, f, parts) in enumerate(plan):
                    b = 5 - n % 2
                    take(b)
                    for e in range(parts):
                        m = piece_b([bank[b][:, e * T:(e + 1) * T]], *U)
                        if e < parts - 1:
                            yield
                    d = dst[:, :] if name == "ik" else dst[:, f:f + 2, :].rearrange("p a n -> p (a n)")
                    m = AC.go((m,), S.activation, d, bank[b][:, 0:parts * T], ACT.Copy)
                    free[b] = (m,)
                    got[name, f] = m
                    yield
                take(0), take(1)
                for g in range(KD // 2):
                    m = piece_a([[bank[0][:, :]], [bank[1][:, :]]], U, (2 * g, 2 * g + 1), 512,
                                g == 0, g == KD // 2 - 1)
                    if g < KD // 2 - 1:
                        yield
                for tt in range(NT):
                    mv = AC.go((m,), S.activation, v_sb[:, tt, :], bank[tt][:, :], ACT.Copy)
                    free[tt] = (mv,)
                got["v"] = mv
                yield
                for f in (0, 2):
                    for name in ("cC", "ch"):
                        b = 4 if name == "cC" else 5
                        take(b)
                        piece_b([bank[b][:, 0:T]], *U)
                        yield
                        m = piece_b([bank[b][:, T:2 * T]], *U)
                        if name == "cC":
                            mc = AC.go((m, got.get("prod")), S.activation, cc[:, 0, :], bank[b][:, :],
                                       ACT.Copy)
                            free[b] = (mc,)
                        else:
                            m = VE.go((m, mc), V.tensor_tensor, prod[:, f:f + 2, TAPS - 1:],
                                      bank[b][:, :].rearrange("p (a n) -> p a n", a=2),
                                      cc[:, 0, :].rearrange("p (a n) -> p a n", a=2), ALU.mult)
                            got["prod"] = m
                            free[b] = (m,)
                        yield
                y_marks = []
                for f in (0, 2):
                    b = 4 + f // 2
                    take(b)
                    piece_b([bank[b][:, 0:T]], *U)
                    for ff in (f, f + 1):
                        m = VE.go((got["prod"], cw_m), V.tensor_scalar, yc[:, ff, :],
                                  prod[:, ff, 0:T], cw[:, ff, 0:1], None, ALU.mult)
                        for j in range(1, TAPS):
                            m = VE.go((m,), V.scalar_tensor_tensor, yc[:, ff, :], prod[:, ff, j:j + T],
                                      cw[:, ff, j:j + 1], yc[:, ff, :], ALU.mult, ALU.add)
                    yield
                    m2 = piece_b([bank[b][:, T:2 * T]], *U)
                    dst = yc[:, f:f + 2, :].rearrange("p a n -> p (a n)")
                    m = VE.go((m, m2), V.tensor_tensor, dst, dst, bank[b][:, :], ALU.mult)
                    free[b] = (m,)
                    y_marks.append(m)
                    yield
                for f in range(0, 2 * KD, 2):
                    b = 4 + (f // 2) % 2
                    take(b)
                    piece_b([bank[b][:, 0:T]], *U)
                    yield
                    m = piece_b([bank[b][:, T:2 * T]], *U)
                    m = AC.go((m,), S.activation, gate[:, f:f + 2, :].rearrange("p a n -> p (a n)"),
                              bank[b][:, :], ACT.Sigmoid)
                    free[b] = (m,)
                    got["gate"] = m
                    yield
                    if f in (2, 4):
                        cols = slice(f - 2, f)
                        got["y"] = split_bank(yc[:, cols, :], y_hi[:, cols, :], y_lo[:, cols, :],
                                              y_marks.pop(0))

            def rope_of(name, dst, f, parts, b):
                n = parts * T
                d = dst[:, :] if name == "ik" else dst[:, f:f + 2, :].rearrange("p a n -> p (a n)")
                PE.wait(got[name, f], (s_rope, 32))
                VE.wait((s_rope, 32))
                take(b)
                t = PE.done(M.matmul(bank[b][:, 0:n], turn[:, :], d, start=True, stop=True))
                r = rot[:, b - 6, 0:n]
                m = VE.go((t, got.get(("rot", b))), V.tensor_tensor, r, bank[b][:, 0:n],
                          rope[:, 1, 0:n], ALU.mult)
                free[b] = (m,)
                m1 = VE.go((t, got[name, f]), V.tensor_tensor, d, d, rope[:, 0, 0:n], ALU.mult)
                m = VE.go((m, m1), V.tensor_tensor, d, d, r, ALU.add)
                got["rot", b] = m
                got[name, f, "r"] = m

            def side_part():
                for _ in range(4):
                    yield
                take(6)
                PE.wait(got["iwT"])
                for tt in range(NT):
                    i = M.transpose(bank[6][:, tt * 32:tt * 32 + 32], iwT[0:32, tt * P:(tt + 1) * P],
                                    ident[0:32, 0:32])
                t = PE.done(i)
                iw_m = VE.go((t,), V.tensor_scalar, iw[:, :, :],
                             bank[6][:, 0:64].rearrange("p (t n) -> p t n", t=2)[:, :, 0:IH],
                             DH ** -0.5 * IH ** -0.5, None, ALU.mult)
                free[6] = (iw_m,)
                rope_of("iq", iqT, 0, 2, 7)
                yield
                rope_of("ik", ikT, 0, 1, 6)
                yield
                for tt in range(NT):
                    nk = (tt + 1) * P
                    PE.wait(got["iq", 0, "r"], got["ik", 0, "r"])
                    b = (2, 3)
                    for h in range(IH):
                        bb = b[h % 2]
                        if h < 2:
                            take(bb)
                        r0 = (h % 2) * DH
                        i = M.matmul(bank[bb][:, (h // 2) * nk:(h // 2 + 1) * nk],
                                     iqT[r0:r0 + DH, h // 2, tt * P:(tt + 1) * P],
                                     ikT[r0:r0 + DH, 0:nk], start=True, stop=True,
                                     skip_group_check=True)
                    t = PE.done(i)
                    m = t
                    sc = score[:, tt, 0:nk]
                    for h in range(IH):
                        src = bank[b[h % 2]][:, (h // 2) * nk:(h // 2 + 1) * nk]
                        dst = sc if h == 0 else work[:, 0, 0:nk]
                        m = VE.go((m, t, iw_m), V.tensor_scalar, dst, src, 0.0, iw[:, tt, h:h + 1],
                                  ALU.max, ALU.mult)
                        if h:
                            m = VE.go((m,), V.tensor_tensor, sc, sc, work[:, 0, 0:nk], ALU.add)
                    free[b[0]] = free[b[1]] = (m,)
                    yield
                    m = VE.go((m,), V.memset, score[0:CHUNK, tt, nk - CHUNK:nk], OUT_OF_BLOCK)
                    src = sc
                    for r in range(TOPK // 8):
                        m = VE.go((m,), V.max, top8[:, :], src)
                        dst = work[:, r % 2, 0:nk]
                        m = VE.go((m,), V.match_replace, dst, top8[:, :], src, TAKEN)
                        src = dst
                        if r % 2:
                            yield
                    bs = sbias[:, tt, 0:nk]
                    m = VE.go((m,), V.tensor_tensor, bs, src, sc, ALU.not_equal)
                    m = VE.go((m,), V.tensor_scalar, bs, bs, -1.0, BIG, ALU.add, ALU.mult)
                    got["bias", tt] = m
                    yield
                rope_of("k", kT, 0, 2, 7)
                yield
                rope_of("k", kT, 2, 2, 6)
                yield
                rope_of("q", qT, 0, 2, 7)
                yield
                rope_of("q", qT, 2, 2, 6)
                yield
                VE.wait((s_t5w, 16))
                ready = [got[n, f, "r"] for n in "qk" for f in (0, 2)] + [got["v"]]
                for tt in range(NT):
                    nk = (tt + 1) * P

                    def rows(tensor, h, cols):
                        return tensor[(h % 2) * DH:(h % 2 + 1) * DH, h // 2, cols]
                    yield from attention(
                        tt, nk, lambda h: rows(qT, h, slice(tt * P, (tt + 1) * P)),
                        lambda h: rows(kT, h, slice(0, nk)),
                        lambda kt, h: v_sb[:, kt, h * DH:(h + 1) * DH],
                        lambda heads: sbias[:, tt, 0:nk].unsqueeze(1).to_broadcast([P, 2, nk]),
                        (got["bias", tt],), buf, o_sb[:, tt, :], ready, SAME_PARITY)
                    yield
                    t = transposes(7, [o_sb[:, tt, k * P:(k + 1) * P] for k in range(KW)],
                                   (buf["done"],))
                    cols = slice(tt * P, (tt + 1) * P)
                    m2, m1 = split_bank(bank[7][:, :].rearrange("p (k n) -> p k n", k=KW),
                                        o_hi[:, :, cols], o_lo[:, :, cols], t)
                    free[7] = (m1, m2)
                    got["o"] = (m1, m2)
                    yield

            weave(main_part(), side_part())
            u_read = (s_used, dyn(RING) + at["piece"])
            PE.wait(*got["o"], *got["y"])
            merged, u_marks = [], []

            def split_merged(g):
                m2, m1 = split_bank(cc[:, g % 2, :].rearrange("p (a n) -> p a n", a=2),
                                    u_hi[:, 2 * g:2 * g + 2, :], u_lo[:, 2 * g:2 * g + 2, :], merged[g],
                                    (u_read,) if g == 0 else ())
                got["cc", g % 2] = m2
                u_marks.append((m1, m2))

            for g in range(KD // 2):
                pb = 4 + g % 2
                pc = 6 + g % 2
                take(pb)
                ma = piece_b([bank[pb][:, 0:T], bank[pb][:, T:2 * T]], o_hi, o_lo, KW, 2)
                take(pc)
                mc = piece_b([bank[pc][:, 0:T], bank[pc][:, T:2 * T]], y_hi, y_lo, KW, 2)
                e = g % 2
                g0 = gate[:, 2 * g:2 * g + 2, :].rearrange("p a n -> p (a n)")
                g1 = gate[:, KD + 2 * g:KD + 2 * g + 2, :].rearrange("p a n -> p (a n)")
                m = VE.go((ma, got["gate"], got.get(("cc", e))), V.tensor_tensor, cc[:, e, :], bank[pb][:, :], g0,
                          ALU.mult)
                free[pb] = (m,)
                m1 = VE.go((mc,), V.tensor_tensor, rot[:, e, :], bank[pc][:, :], g1, ALU.mult)
                free[pc] = (m1,)
                m = VE.go((m, m1), V.tensor_tensor, cc[:, e, :], cc[:, e, :], rot[:, e, :], ALU.add)
                merged.append(m)
                if g:
                    split_merged(g - 1)
            split_merged(KD // 2 - 1)
            acc = acc_banks()
            for k in range(KD):
                PE.wait(*u_marks[k // 2])
                m = piece_a(acc, U, (k,), D, k == 0, k == KD - 1)
            m = add_to_x(x, m)
            VE.wait((s_gain, 16))
            run(norm_to_u(x, xn, gains[:, bass.ds(layer * 1 + LAYERS, 1), :].rearrange(
                "p a n -> p (a n)"), m))
            acc = acc_banks()
            take(4), take(5)

            def up(q, tile, first=False):
                if not first:
                    nc.tensor.wait_ge(s_act, (tile - 2) * 3 + 1)
                m = piece_b([bank[4 + q][:, 0:T]], *U)
                nc.scalar.wait_ge(*m)
                if not first:
                    nc.scalar.wait_ge(s_act, (tile - 2) * 3 + 3)
                nc.scalar.activation(relu[:, q, :], bank[4 + q][:, 0:T], ACT.Relu).then_inc(s_relu, 1)
                nc.vector.wait_ge(s_relu, tile + 1)
                nc.vector.tensor_tensor(relu[:, q, :], relu[:, q, :], bank[4 + q][:, 0:T],
                                        ALU.mult).then_inc(s_act, 1)
                nc.vector.wait_ge(s_act, tile * 3 + 1)
                if not first:
                    nc.vector.wait_ge(s_used, m[1] + 1)
                nc.vector.tensor_copy(a_hi[:, q, :], relu[:, q, :]).then_inc(s_act, 1)
                nc.vector.wait_ge(s_act, tile * 3 + 2)
                nc.vector.tensor_tensor(a_lo[:, q, :], relu[:, q, :], a_hi[:, q, :].bitcast(F32),
                                        ALU.subtract).then_inc(s_act, 1)

            def down(q, tile, first, last):
                nc.tensor.wait_ge(s_act, tile * 3 + 3)
                s = next_piece()
                for tt in range(NT):
                    for n in range(2):
                        i = mm3(acc[tt][n], a_hi[:, q, tt * P:(tt + 1) * P],
                                a_lo[:, q, tt * P:(tt + 1) * P], w_hi[:, s, n * 512:(n + 1) * 512],
                                w_lo[:, s, n * 512:(n + 1) * 512], first, last)
                return used(i)

            tile0 = layer * KH
            up(0, tile0 + 0, True)
            up(1, tile0 + 1, True)
            for q in range(2):
                up(q, tile0 + 2 + q)
                down(q, tile0 + q, q == 0, False)
            base = at["piece"]
            quads = at["quads"]
            with nc.Fori(0, KH // 2 - 2, engines=compute) as i:
                at["quads"] = quads + i
                for q in range(2):
                    up(q, tile0 + i * 2 + (4 + q))
                    down(q, tile0 + i * 2 + (2 + q), False, False)
            at["quads"], at["piece"] = quads, base + (KH - 4) * 2
            for q in range(2):
                m = down(q, tile0 + KH - 2 + q, False, q == 1)
            run(row_scales(x, xn, add_to_x(x, m)))
            assert at["piece"] == N_LAYER
        at["quads"], at["piece"] = 0, LAYERS * N_LAYER
        restart_lines()
        ph1a.close()

        ph1b = ph1.enter_context(ExitStack())
        gains_b = sb(ph1b, "gains_b", [P, 4, D])
        ada = sb(ph1b, "ada", [P, 6, D])
        bias_a, bias_b = sb(ph1b, "bias_a", [P, H, BIAS_W]), sb(ph1b, "bias_b", [P, H, BIAS_W])
        na_mask = sb(ph1b, "na_mask", [P, GRID_W])
        sink = sb(ph1b, "sink", [P, H])
        kaT, vaT = sb(ph1b, "kaT", [P, T]), sb(ph1b, "vaT", [P, T])
        va = sb(ph1b, "va", [P, NT, P])
        qbT = sb(ph1b, "qbT", [P, KW, T])
        ob_sb = sb(ph1b, "ob_sb", [P, NT, W])
        p2, rows2 = sb(ph1b, "p2", [P, H, T]), sb(ph1b, "rows2", [P, 5, H])
        junk = sb(ph1b, "junk", [P, 2, W])

        def after_tile(n):
            G.wait_ge(s_relu, (LAYERS - 1) * KH + n)
        after_tile(1)
        G.wait_ge(s_naw, 16)
        G.wait_ge(s_t5w, 32)
        G.dma_start(gains_b[:, :, :], gains2.partition_broadcast(P)).then_inc(s_gain2, 16)
        for g in range(6):
            after_tile(4 + 2 * g)
            G.dma_start(ada[:, g, :], b_ada[g:g + 1, :].partition_broadcast(P).rearrange(
                "p a n -> p (a n)")).then_inc(s_bada, 16)
        after_tile(16)
        G.dma_start(bias_a[:, :, :], bass.AP(tensor=t5_rows.tensor, offset=P - 1,
                                             ap=[[H * T5_W - 1, P], [T5_W, H], [1, BIAS_W]])
                    ).then_inc(s_t5b, 16)
        G.dma_start(na_mask[:, :], na_mask_in).then_inc(s_na, 16)
        G.dma_start(sink[:, :], sinks.partition_broadcast(P)).then_inc(s_sink, 16)
        row = H * NA_DR * P
        for half in range(2):
            for h in range(H):
                if h % 2 == 0:
                    after_tile(18 + 4 * half + h // 2)
                G.dma_start(
                    bias_b[half * GRID_W:(half + 1) * GRID_W, h, :].rearrange("p (q c) -> p q c", c=GRID_W),
                    bass.AP(tensor=rpb_rows.tensor, offset=(h * NA_DR + 1 - half) * P + GRID_W - 1,
                            ap=[[row - 1, GRID_W], [P, BIAS_W // GRID_W], [1, GRID_W]])).then_inc(s_na, 16)

        def ada_group(g):
            b = (4, 5)
            take(b[0]), take(b[1])
            for k in range(KD):
                s = next_piece()
                for n in range(2):
                    i = mm3(bank[b[n]][:, :], c_hi[:, k:k + 1].to_broadcast([P, P]),
                            c_lo[:, k:k + 1].to_broadcast([P, P]),
                            w_hi[:, s, n * 512:(n + 1) * 512], w_lo[:, s, n * 512:(n + 1) * 512],
                            k == 0, k == KD - 1)
                m = used(i)
                if k < KD - 1:
                    yield
            for n in range(2):
                cols = ada[:, g, n * 512:(n + 1) * 512]
                mm = VE.go((m, (s_bada, 96)), V.tensor_tensor, cols, cols, bank[b[n]][:, :], ALU.add)
                free[b[n]] = (mm,)
            got["ada", g] = mm
            yield

        got = {}

        def first_norms():
            for tt in range(NT):
                m = VE.go((scales[0], (s_gain2, 16)), V.scalar_tensor_tensor, x[:, tt, :], x[:, tt, :],
                          st[:, 3, tt:tt + 1], gains_b[:, 0, :], ALU.mult, ALU.mult)
                got["x", tt] = m
                yield
            yield from row_scales(x, xn, [[got["x", tt]] * 2 for tt in range(NT)])

        def next_norm():
            m = VE.go((got["ada", 1], (s_gain2, 16)), V.scalar_tensor_tensor, ada[:, 1, :],
                      ada[:, 1, :], 1.0, gains_b[:, 1, :], ALU.add, ALU.mult)
            VE.wait(m)
            yield from scaled_to_u(x, xn, ada[:, 1, :], ada[:, 0, :])
            bb = bias_b[:, :, :].rearrange("p h (q c) -> p (h q) c", c=GRID_W)
            got["bias_b"] = VE.go(
                ((s_na, 16 * (1 + 2 * H)),), V.tensor_tensor, bb, bb,
                na_mask[:, :].unsqueeze(1).to_broadcast([P, H * BIAS_W // GRID_W, GRID_W]), ALU.add)

        def ada_groups(*groups):
            for g in groups:
                yield from ada_group(g)

        weave(ada_groups(0, 1), first_norms())
        weave(ada_groups(2), next_norm())
        U = (u_hi, u_lo)
        buf.pop("p_free", None), buf.pop("pt_free", None)
        buf2 = {"p": p2, "pt": xn[:, :, :].rearrange("p t (h n) -> p t h n", h=H), "rows": rows2,
                "score_banks": (2, 3, 2, 3), "turn_banks": (7, 2)}
        buf["score_banks"], buf["turn_banks"] = (0, 1, 0, 1), (6, 0)
        LAG = 2

        def main2():
            plan = [(kaT, None, 1, "ka"), (qT, 0, 2, "qa"), (qT, 2, 2, "qa"), (vaT, None, 1, "va"),
                    (kT, 0, 2, "kb"), (kT, 2, 2, "kb"), (qbT, 0, 2, "qb"), (qbT, 2, 2, "qb")]
            for n, (dst, f, parts, name) in enumerate(plan):
                b = 4 + n % 2
                take(b)
                for e in range(parts):
                    m = piece_b([bank[b][:, e * T:(e + 1) * T]], *U)
                    if e < parts - 1:
                        yield
                d = dst[:, :] if f is None else dst[:, f:f + 2, :].rearrange("p a n -> p (a n)")
                m = AC.go((m,), S.activation, d, bank[b][:, 0:parts * T], ACT.Copy)
                free[b] = (m,)
                got[name] = m
                yield
            take(4), take(5)
            for g in range(KD // 2):
                m = piece_a([[bank[4][:, :]], [bank[5][:, :]]], U, (2 * g, 2 * g + 1), 512,
                            g == 0, g == KD // 2 - 1)
                if g < KD // 2 - 1:
                    yield
            for tt in range(NT):
                mv = AC.go((m,), S.activation, v_sb[:, tt, :], bank[4 + tt][:, :], ACT.Copy)
                free[4 + tt] = (mv,)
            got["vb"] = mv
            got["u_read"] = m
            yield
            yield from ada_groups(3, 4)

        def mixed(tt, src, k0, cols, buf, c):
            sst = st[:, :, c:c + 1]
            m = AC.go((buf["done"],), S.activation, junk[:, c, :], src[:, tt, :], ACT.Square,
                      accum_out=sst[:, 0, :])
            ss_marks[:] = [m]
            m = inverse_root(sst, W, 1)
            yield
            m = VE.go((m, (s_gain2, 16)), V.scalar_tensor_tensor, src[:, tt, :], src[:, tt, :],
                      sst[:, 3, :], gains_b[:, 3, cols], ALU.mult, ALU.mult)
            yield
            b = buf["turn_banks"][0]
            t = transposes(b, [src[:, tt, k * P:(k + 1) * P] for k in range(KW)], (m,))
            rows = slice(tt * P, (tt + 1) * P)
            m2, m1 = split_bank(bank[b][:, :].rearrange("p (k n) -> p k n", k=KW),
                                u_hi[:, k0:k0 + KW, rows], u_lo[:, k0:k0 + KW, rows], t,
                                (got["u_read"],))
            free[b] = (m1, m2)
            got.setdefault("mix", []).append((m1, m2))
            yield

        def va_part():
            take(7)
            PE.wait(got["va"])
            for tt in range(NT):
                i = M.transpose(bank[7][:, tt * P:(tt + 1) * P], vaT[:, tt * P:(tt + 1) * P], ident)
            t = PE.done(i)
            va_mark = VE.go((t,), V.tensor_copy, va[:, :, :].rearrange("p a n -> p (a n)"),
                            bank[7][:, 0:NT * P])
            free[7] = (va_mark,)
            got["vat"] = va_mark

        def bias_of(table, tt):
            return lambda heads: table[:, heads, P * (1 - tt):P * (1 - tt) + T]

        def chain(tt, buf):
            yield from attention(
                tt, T,
                lambda h: qT[(h // 4) * DH:(h // 4 + 1) * DH, h % 4, tt * P:(tt + 1) * P],
                lambda h: kaT[(h // 4) * DH:(h // 4 + 1) * DH, :],
                lambda kt, h: va[:, kt, (h // 4) * DH:(h // 4 + 1) * DH],
                bias_of(bias_a, tt), ((s_t5b, 16),), buf, o_sb[:, tt, :],
                (got["qa"], got["ka"], got["vat"]), SAME_GROUP, sink[:, :])
            yield
            while "u_read" not in got:
                yield
            yield from mixed(tt, o_sb, 0, slice(0, W), buf, tt)
            yield from attention(
                tt, T,
                lambda h: qbT[(h % 2) * DH:(h % 2 + 1) * DH, h // 2, tt * P:(tt + 1) * P],
                lambda h: kT[(h % 2) * DH:(h % 2 + 1) * DH, h // 2, :],
                lambda kt, h: v_sb[:, kt, h * DH:(h + 1) * DH],
                bias_of(bias_b, tt), (got["bias_b"],), buf, ob_sb[:, tt, :],
                (got["qb"], got["kb"], got["vb"]), SAME_PARITY)
            yield
            yield from mixed(tt, ob_sb, KW, slice(W, 2 * W), buf, tt)

        def side2():
            for _ in range(7):
                yield
            va_part()
            chains = [chain(0, buf), chain(1, buf2)]
            for n in range(1000):
                for c in range(2):
                    if c == 0 or n >= LAG:
                        if chains[c] is not None and next(chains[c], "end") == "end":
                            chains[c] = None
                if chains == [None, None]:
                    return
                yield

        VE.wait((s_sink, 16))
        weave(main2(), side2())
        PE.wait(*(m for marks in got["mix"] for m in marks))
        acc = acc_banks()
        for k in range(KD):
            m = piece_a(acc, U, (k,), D, k == 0, k == KD - 1)
        last = m
        x_marks = [[None, None], [None, None]]
        for tt in range(NT):
            for n in range(2):
                cols = slice(n * 512, (n + 1) * 512)
                b = 2 * tt + n
                m = VE.go((last, got["ada", 4]), V.tensor_tensor, xn[:, tt, cols], bank[b][:, :],
                          ada[:, 2, cols], ALU.mult)
                free[b] = (m,)
                m = VE.go((m,), V.tensor_tensor, x[:, tt, cols], x[:, tt, cols], xn[:, tt, cols], ALU.add)
                x_marks[tt][n] = m
        AC.wait(m)
        S.dma_start(x_dram.rearrange("t p d -> p t d"), x[:, :, :]).then_inc(s_park, 16)

        def second_norm():
            m = VE.go((), V.scalar_tensor_tensor, ada[:, 4, :], ada[:, 4, :], 1.0, gains_b[:, 2, :],
                      ALU.add, ALU.mult)
            VE.wait(m)
            yield from norm_to_u(x, xn, ada[:, 4, :], x_marks, ada[:, 3, :])
        weave(ada_groups(5), second_norm())
        AC.wait((s_bada, 96), got["ada", 5])
        S.dma_start(gate_dram, ada[0:1, 5, :]).then_inc(s_park, 16)
        ph1.close()
        Z = sb(ctx, "Z", [P, PK * T])
        sel = sb(ctx, "sel", [P, 3, T])
        GROUP = 4
        rows_a = sb(ctx, "rows_a", [P, 2, GROUP, P])
        rows_b = sb(ctx, "rows_b", [P, 2, GROUP, FIRST])
        qhT = Z[:, 0:N_QUERY * T].rearrange("p (f t) -> p f t", t=T)
        skT = Z[:, N_QUERY * T:N_QUERY * (T + PK)].rearrange("p (f n) -> p f n", n=PK)
        at_tail = [PH * SEL_PIECES * T]

        def tail(n):
            at_tail[0] += n
            assert at_tail[0] <= PK * T
            return Z[:, at_tail[0] - n:at_tail[0]]
        scores = tail(PH * 4 * PK).rearrange("p (h n) -> p h n", h=PH)
        hs, hs2, cand, cand2, eq = tail(512), tail(512), tail(512), tail(512), tail(512)
        val = tail(64).rearrange("p (a n) -> p a n", a=4)
        idx = tail(64).rearrange("p (a n) -> p a n", a=4)
        idxf = tail(64).rearrange("p (t s n) -> p t s n", t=2, s=2)
        pick = tail(64).rearrange("p (a n) -> p a n", a=2)
        pick_hl, pick_f = tail(64), tail(64)
        best = tail(NT * P).rearrange("p (t n) -> p t n", t=NT)
        rowcol = tail(2 * NT * P).rearrange("p (s t n) -> p s t n", s=2, t=NT)
        smx = tail(2 * NT * PH).rearrange("p (a n) -> p a n", a=2)

        AC.wait((s_park, 32))
        VE.wait((s_park, 32))
        for f in range(0, N_QUERY, 2):
            b = 4 + (f // 2) % 2
            take(b)
            piece_b([bank[b][:, 0:T]], *U)
            m = piece_b([bank[b][:, T:2 * T]], *U)
            m = AC.go((m,), S.activation, qhT[:, f:f + 2, :].rearrange("p a n -> p (a n)"),
                      bank[b][:, :], ACT.Copy)
            free[b] = (m,)
            if f == 0:
                S.dma_start(skT, sub_keys).then_inc(s_sk, 16)
        PE.wait(m, (s_sk, 16))
        for h in range(PH):
            b = h % 4
            take(b)
            for tt in range(NT):
                for side in range(2):
                    i = M.matmul(bank[b][:, (2 * tt + side) * PK:(2 * tt + side + 1) * PK],
                                 qhT[:, 2 * h + side, tt * P:(tt + 1) * P], skT[:, 2 * h + side, :],
                                 start=True, stop=True, skip_group_check=True)
            t = PE.done(i)
            m = VE.go((t,), V.tensor_copy, scores[:, h, :], bank[b][:, :])
            free[b] = (m,)
        take(0), take(1), take(2), take(3), take(4), take(5)
        VE.wait(m)
        CH = Line(nc.vector, s_chain)
        S.sem_inc(s_z, 2)

        def expert_up(q, tile):
            nc.tensor.wait_ge(s_z, tile + 1)
            m = piece_b([bank[4 + q][:, 0:T]], *U)
            nc.scalar.wait_ge(*m)
            nc.scalar.activation(Z[:, bass.ds(tile * T, T)], bank[4 + q][:, 0:T],
                                 ACT.Gelu_apprx_tanh).then_inc(s_z, 1)

        def top16(rows_of, m):
            m0 = [m] * len(rows_of)
            for r in range(2):
                half = slice(8 * r, 8 * r + 8)
                if r:
                    for a, (src, spare, v, ix) in enumerate(rows_of):
                        m0[a] = CH.go((m0[a],), V.match_replace, spare, v[:, 0:8], src, TAKEN)
                for a, (src, spare, v, ix) in enumerate(rows_of):
                    m0[a] = CH.go((m0[a],), V.max, v[:, half], spare if r else src)
                for a, (src, spare, v, ix) in enumerate(rows_of):
                    m = CH.go((m0[a],), V.max_index, ix[:, half], v[:, half], spare if r else src)
                yield
            got["chain"] = m

        def select(h):
            m = CH.go((), V.tensor_copy, hs, scores[:, bass.ds(h, 1), :].rearrange("p a n -> p (a n)"))
            for a2 in (0, 2):
                yield from top16([(hs[:, a * PK:(a + 1) * PK], hs2[:, a * PK:(a + 1) * PK],
                                   val[:, a, :], idx[:, a, :].bitcast(U32)) for a in (a2, a2 + 1)], m)
            m = got["chain"]
            m1 = CH.go((m,), V.tensor_copy, idxf.rearrange("p t s n -> p (t s n)"),
                       idx.rearrange("p a n -> p (a n)").bitcast(U32))
            v4 = val.rearrange("p (t s) n -> p t s n", s=2)
            for tt in range(NT):
                m = CH.go((m,), V.tensor_tensor,
                          cand[:, tt * 256:(tt + 1) * 256].rearrange("p (i j) -> p i j", j=PT),
                          v4[:, tt, 0, :].unsqueeze(2).to_broadcast([P, PT, PT]),
                          v4[:, tt, 1, :].unsqueeze(1).to_broadcast([P, PT, PT]), ALU.add)
            yield
            yield from top16([(cand[:, tt * 256:(tt + 1) * 256], cand2[:, tt * 256:(tt + 1) * 256],
                               pick[:, 0, tt * PT:(tt + 1) * PT],
                               pick[:, 1, tt * PT:(tt + 1) * PT].bitcast(U32)) for tt in range(NT)], m)
            m = got["chain"]
            places = pick[:, 1, :].bitcast(U32)
            CH.go((m,), V.tensor_scalar, pick_hl[:, 0:32].bitcast(U32), places, 4, None,
                  ALU.logical_shift_right)
            m2 = CH.go((m,), V.tensor_scalar, pick_hl[:, 32:64].bitcast(U32), places, 15, None,
                       ALU.bitwise_and)
            CH.go((m,), V.tensor_copy, best[:, :, bass.ds(h * PT, PT)],
                  pick[:, 0, :].rearrange("p (t n) -> p t n", t=NT))
            m = CH.go((m2, m1), V.tensor_copy, pick_f, pick_hl.bitcast(U32))
            yield
            e5 = [eq.rearrange("p (t k m) -> p t k m", t=NT, k=PT),
                  cand2.rearrange("p (t k m) -> p t k m", t=NT, k=PT)]
            jobs = [(side, tt) for side in range(2) for tt in range(NT)]
            ms = [CH.go((m,), V.tensor_tensor, e5[side][:, tt],
                        pick_f[:, 32 * side + PT * tt:32 * side + PT * (tt + 1)].unsqueeze(2).to_broadcast(
                            [P, PT, PT]),
                        iota16.unsqueeze(1).to_broadcast([P, PT, PT]), ALU.is_equal)
                  for side, tt in jobs]
            yield
            ms = [CH.go((ms[n],), V.tensor_tensor, e5[side][:, tt], e5[side][:, tt],
                        idxf[:, tt, side, :].unsqueeze(1).to_broadcast([P, PT, PT]), ALU.mult)
                  for n, (side, tt) in enumerate(jobs)]
            yield
            for side in range(2):
                CH.go((ms[2 * side + 1],), V.tensor_reduce, rowcol[:, side, :, bass.ds(h * PT, PT)],
                      e5[side], AX.X, ALU.add)
                yield

        quads0, piece0 = at["quads"], at["piece"]
        with nc.Fori(0, PH, engines=compute) as h:
            at["quads"], at["piece"] = quads0 + h * (SEL_PIECES // RING), piece0
            CH.restart()

            def ups():
                for j in range(SEL_PIECES):
                    expert_up(j % 2, h * SEL_PIECES + j)
                    yield
            weave(ups(), select(h), 2)
            nc.vector.wait_ge(s_chain, CH.n)
            nc.vector.sem_clear(s_chain)
        at["quads"], at["piece"] = quads0, piece0 + PH * SEL_PIECES
        n0 = PH * SEL_PIECES

        def weigh():
            b4 = best.rearrange("p t (h k) -> p (t h) k", k=PT)
            m = VE.go((), V.tensor_tensor, cand[:, 0:NT * P].rearrange("p (g k) -> p g k", k=PT), b4,
                      b4[:, :, 0:1].to_broadcast([P, NT * PH, PT]), ALU.subtract)
            m = AC.go((m,), S.activation, best.rearrange("p t n -> p (t n)"), cand[:, 0:NT * P], ACT.Exp)
            yield
            m = VE.go((m,), V.tensor_reduce, smx[:, 0, :], b4, AX.X, ALU.add)
            m = VE.go((m,), V.reciprocal, smx[:, 1, :], smx[:, 0, :])
            m = VE.go((m,), V.tensor_tensor, b4, b4, smx[:, 1, :].unsqueeze(2).to_broadcast(
                [P, NT * PH, PT]), ALU.mult)
            yield
            PE.wait(m)
            for a, src in enumerate((best, rowcol[:, 0, :, :], rowcol[:, 1, :, :])):
                for tt in range(NT):
                    i = M.transpose(bank[a][:, tt * P:(tt + 1) * P], src[:, tt, :], ident)
            t = PE.done(i)
            yield
            for a in range(3):
                m = VE.go((t,), V.tensor_copy, sel[:, a, :], bank[a][:, 0:T])
            got["sel"] = m
            yield

        def ups2():
            for j in range(RING):
                expert_up(j % 2, n0 + j)
                yield
        scores_read = VE.done(V.memset(rows_a[:, 0, 0, 0:1], 0.0))
        AC.wait(scores_read)
        weave(ups2(), weigh())
        AC.wait(got["sel"])
        VE.wait(got["sel"])

        byt = Z[:, :].rearrange("p (j t) -> p t j", t=T)
        total = T // GROUP

        def rows(q, g, cols):
            n = cols.stop - cols.start
            for e in range(GROUP):
                V.tensor_scalar(rows_a[:, q, e, :], iota, sel[:, 1, bass.ds(g * GROUP + e, 1)],
                                sel[:, 0, bass.ds(g * GROUP + e, 1)], ALU.is_equal, ALU.mult)
            V.tensor_tensor(rows_b[:, q, :, 0:n], iota[:, cols].unsqueeze(1).to_broadcast([P, GROUP, n]),
                            sel[:, 2, bass.ds(g * GROUP, GROUP)].unsqueeze(2).to_broadcast([P, GROUP, n]),
                            ALU.is_equal).then_inc(s_ha, 1)

        def maps(q, g, done, cols, ahead=True):
            n = cols.stop - cols.start
            if ahead:
                rows(1 - q, g + 1, cols)
            M.wait_ge(s_ha, g + (done + 1))
            for e in range(GROUP):
                ins = M.matmul(bank[6 + q][:, e * n:(e + 1) * n], rows_a[:, q, e, :],
                               rows_b[:, q, e, 0:n], start=True, stop=True, skip_group_check=True)
            ins.then_inc(s_g, 1)

        def apply(q, g, done, cols):
            n = cols.stop - cols.start
            V.wait_ge(s_g, g + (done + 1))
            zt = byt[:, bass.ds(g * GROUP, GROUP), cols]
            V.tensor_tensor(zt, zt, bank[6 + q][:, 0:GROUP * n].rearrange("p (t j) -> p t j", t=GROUP),
                            ALU.mult).then_inc(s_m, 1)

        left, right = slice(0, FIRST), slice(FIRST, PK)
        take(6), take(7)
        V.wait_ge(s_z, FIRST + 2)
        rows(0, 0, left)
        for g in range(2 * RING):
            if g % 2 == 0:
                expert_up((g // 2) % 2, FIRST + g // 2)
            if g:
                apply((g - 1) % 2, g - 1, 0, left)
            maps(g % 2, g, 0, left)
        quads, piece = at["quads"], at["piece"]
        with nc.Fori(0, (PK - FIRST) // RING - 2, engines=compute) as i:
            at["quads"], at["piece"] = quads + i, piece
            for j in range(RING):
                expert_up(j % 2, i * RING + (FIRST + RING + j))
                apply((j - 1) % 2, i * RING + (2 * RING + j - 1), 0, left)
                maps(j % 2, i * RING + (2 * RING + j), 0, left)
        at["quads"], at["piece"] = quads, piece + PK - FIRST - 2 * RING
        for j in range(RING):
            expert_up(j % 2, PK - RING + j)
            apply((j - 1) % 2, total - RING + j - 1, 0, left)
            maps(j % 2, total - RING + j, 0, left, j < RING - 1)
        apply(1, total - 1, 0, left)
        assert (PK - FIRST) + RING == total
        V.wait_ge(s_z, PK + 2)

        S.wait_ge(s_m, total)

        def weighted(q, tile, read):
            zj = Z[:, bass.ds(tile * T, T)]
            if read is not None:
                S.wait_ge(s_used, read)
            S.activation(a_hi[:, q, :], zj, ACT.Copy).then_inc(s_ah, 1)
            V.wait_ge(s_ah, tile + 1)
            V.tensor_tensor(a_lo[:, q, :], zj, a_hi[:, q, :].bitcast(F32), ALU.subtract).then_inc(s_al, 1)

        def expert_down(q, tile, first=False, last=False, more=True):
            if more:
                weighted(1 - q, tile + 1, dyn(RING) + at["piece"])
            s = next_piece(at["piece"] + AHEAD >= N_PIECES)
            M.wait_ge(s_al, tile + 1)
            for tt in range(NT):
                for n in range(2):
                    ins = mm3(acc[tt][n], a_hi[:, q, tt * P:(tt + 1) * P],
                              a_lo[:, q, tt * P:(tt + 1) * P], w_hi[:, s, n * 512:(n + 1) * 512],
                              w_lo[:, s, n * 512:(n + 1) * 512], first, last)
            return used(ins)

        acc = [[bank[0][:, :], bank[1][:, :]], [bank[2][:, :], bank[3][:, :]]]
        weighted(0, 0, None)
        rows(0, 0, right)
        for j in range(RING):
            expert_down(j % 2, j, first=j == 0)
            if j:
                apply((j - 1) % 2, j - 1, total, right)
            maps(j % 2, j, total, right)
        quads, piece = at["quads"], at["piece"]
        with nc.Fori(0, total // RING - 2, engines=compute) as i:
            at["quads"], at["piece"] = quads + i, piece
            for j in range(RING):
                expert_down(j % 2, i * RING + (RING + j))
                apply((j - 1) % 2, i * RING + (RING + j - 1), total, right)
                maps(j % 2, i * RING + (RING + j), total, right)
        at["quads"], at["piece"] = quads, piece + total - 2 * RING
        for j in range(RING):
            expert_down(j % 2, total - RING + j)
            apply((j - 1) % 2, total - RING + j - 1, total, right)
            maps(j % 2, total - RING + j, total, right, j < RING - 1)
        apply(1, total - 1, total, right)
        S.wait_ge(s_m, 2 * total)
        quads, piece = at["quads"], at["piece"]
        with nc.Fori(0, (PK - total) // RING - 1, engines=compute) as i:
            at["quads"], at["piece"] = quads + i, piece
            for j in range(RING):
                expert_down(j % 2, i * RING + (total + j))
        at["quads"], at["piece"] = quads, piece + PK - total - RING
        S.wait_ge(s_used, N_PIECES - PK // 2)
        S.wait_ge(s_al, PK // 2)
        xr = Z[:, 0:NT * D].rearrange("p (t n) -> p t n", t=NT)
        g2, gf = Z[:, NT * D:(NT + 1) * D], Z[:, (NT + 1) * D:(NT + 2) * D]
        yo = Z[:, (NT + 2) * D:(2 * NT + 2) * D].rearrange("p (t n) -> p t n", t=NT)
        S.dma_start(xr, x_dram.rearrange("t p d -> p t d")).then_inc(s_back, 16)
        S.dma_start(g2, gate_dram.partition_broadcast(P).rearrange("p a n -> p (a n)")).then_inc(s_back, 16)
        S.dma_start(gf, gain_out.partition_broadcast(P).rearrange("p a n -> p (a n)")).then_inc(s_back, 16)
        for j in range(RING):
            n = PK - RING + j
            m = expert_down(j % 2, n, last=j == RING - 1, more=j < RING - 1)
        assert at["piece"] == N_PIECES, (at["piece"], N_PIECES)
        VE.wait((s_back, 48))
        S.wait_ge(s_back, 48)
        marks = [[None, None], [None, None]]
        for tt in range(NT):
            for n in range(2):
                cols = slice(n * 512, (n + 1) * 512)
                m1 = VE.go((m,), V.tensor_tensor, yo[:, tt, cols], bank[2 * tt + n][:, :], g2[:, cols],
                           ALU.mult)
                marks[tt][n] = VE.go((m1,), V.tensor_tensor, xr[:, tt, cols], xr[:, tt, cols],
                                     yo[:, tt, cols], ALU.add)
        run(row_scales(xr, yo, marks))
        m = scales[0]
        for tt in range(NT):
            for n in range(2):
                cols = slice(n * 512, (n + 1) * 512)
                m1 = VE.go((m,), V.scalar_tensor_tensor, yo[:, tt, cols], xr[:, tt, cols],
                           st[:, 3, tt:tt + 1], gf[:, cols], ALU.mult, ALU.mult)
                nc.sync.wait_ge(*m1)
                nc.sync.dma_start(out[tt * P:(tt + 1) * P, cols], yo[:, tt, cols]).then_inc(s_out, 16)
        nc.sync.wait_ge(s_out, 16 * NT * 2)


def pieces_b(w):
    k, f = w.shape[0] // P, w.shape[1] // P
    return w.reshape(k, P, f, P).transpose(2, 1, 0, 3).reshape(f, P, k * P)


def pieces_b4(w):
    return w.reshape(KW, P, KD // 2, 2, P).transpose(2, 1, 3, 0, 4).reshape(KD // 2, P, PIECE)


def pieces_a(w):
    return w.reshape(-1, P, w.shape[1])


def pieces_v(w):
    return w.reshape(KD // 2, 2, P, W).transpose(0, 2, 1, 3).reshape(KD // 2, P, PIECE)


def interleaved(up, down):
    order = [up[0], up[1]]
    for j in range(KH - 2):
        order += [up[j + 2], down[j]]
    return np.stack(order + [down[KH - 2], down[KH - 1]])


def weight_stream(a):
    parts = []
    cuts = np.cumsum([W, W, W, IH * DH, DH, IH, W, W, W, 2 * D])
    for l in range(LAYERS):
        q, k, v, iq, ik, iw, cb, cc, ch, g = np.split(a["w_in"][l], cuts[:-1], axis=1)
        parts += [pieces_b(np.concatenate([iw, np.zeros((D, P - IH), np.float32)], 1)), pieces_b(iq),
                  pieces_b(np.concatenate([ik, ik], 1)), pieces_b(k), pieces_b(q), pieces_v(v)]
        cc, ch = pieces_b(cc), pieces_b(ch)
        parts += [cc[0:2], ch[0:2], cc[2:4], ch[2:4], pieces_b(cb), pieces_b(g)]
        pair = np.stack([pieces_b4(a["w_attn_out"][l]), pieces_b4(a["w_conv_out"][l])], 1)
        parts += [pair.reshape(-1, P, PIECE), pieces_a(a["w_mix_out"][l]),
                  interleaved(pieces_b(a["w_mlp_up"][l]), pieces_a(a["w_mlp_down"][l]))]
    ada = a["w_ada_2"][0].reshape(KD, P, 6, D).transpose(2, 0, 1, 3)
    qa, ka, va, qb, kb, vb = np.split(a["w_in_2"][0], np.cumsum([W, P, P, W, W]), axis=1)
    qa = qa.reshape(D, 2, KW, DH).transpose(0, 2, 1, 3).reshape(D, W)
    parts += [ada[0:3].reshape(-1, P, D), pieces_b(ka), pieces_b(qa), pieces_b(va), pieces_b(kb), pieces_b(qb),
              pieces_v(vb), ada[3:5].reshape(-1, P, D), pieces_a(a["w_out_2"][0]), ada[5],
              pieces_b(a["w_query_2"][0])]
    u = a["u_experts_2"][0].reshape(PK, PK, KD, P).transpose(1, 3, 2, 0).reshape(PK, P, PIECE)
    v = a["v_experts_2"][0].reshape(PK, P, D).transpose(1, 0, 2)
    return np.concatenate(parts + [u, v])


def kept_table():
    row = np.arange(P, dtype=np.float32)
    return np.concatenate([np.eye(P, dtype=np.float32), np.tile(row, (P, 1)),
                           np.tile(row[:PT], (P, 1))], 1)


def rope_table():
    half = ROPE // 2
    inv = (1.0 / (np.float32(ROPE_THETA) ** (np.arange(0, ROPE, 2, dtype=np.float32) / ROPE))
           ).astype(np.float32)
    ang = np.arange(T, dtype=np.float32)[:, None] * inv[None, :]
    cos, sin = np.ones((P, T), np.float32), np.zeros((P, T), np.float32)
    turn = np.zeros((P, P), np.float32)
    for f in range(P):
        d = f % DH
        if d < ROPE:
            cos[f] = np.cos(ang[:, d % half])
            sin[f] = np.sin(ang[:, d % half]) * (-1.0 if d < half else 1.0)
            turn[f + half if d < half else f - half, f] = 1.0
    return np.concatenate([cos, cos, sin, sin, turn], 1)


def t5_table_of_distance():
    rel = np.arange(T5_W) - (T - 1)
    half, exact = T5_BUCKETS // 2, T5_BUCKETS // 4
    n = np.abs(rel)
    nf = np.maximum(n, 1).astype(np.float32)
    large = exact + (np.log(nf / np.float32(exact)) / np.float32(np.log(T5_MAX / exact))
                     * (half - exact)).astype(np.int32)
    bucket = np.where(rel > 0, half, 0) + np.where(n < exact, n, np.minimum(large, half - 1))
    hot = np.zeros((DH, T5_W), np.float32)
    inside = n <= WINDOW
    hot[bucket[inside], np.arange(T5_W)[inside]] = 1.0
    hot[T5_BUCKETS, ~inside] = -BIG
    return hot


def na_column_mask():
    c = np.arange(GRID_W)
    start = np.clip(c - NA_COLS // 2, 0, GRID_W - NA_COLS)
    seen = (c[None, :] >= start[:, None]) & (c[None, :] < start[:, None] + NA_COLS)
    return np.tile(np.where(seen, 0.0, -BIG).astype(np.float32), (2, 1))


def kernel(**inputs):
    import concourse.bacc as bacc
    from concourse.bass_utils import run_bass_kernel_spmd

    a = {k: np.asarray(v) for k, v in inputs.items()}
    t5 = np.zeros((DH, H), np.float32)
    t5[0:T5_BUCKETS], t5[T5_BUCKETS] = a["t5_table_2"], 1.0
    rpb = np.zeros((H, 2 * NA_ROWS - 1, P), np.float32)
    rpb[:, :, GRID_W - NA_COLS:GRID_W + NA_COLS - 1] = a["rpb_b_2"][0]
    arrays = {
        "stream": weight_stream(a),
        "x_in": a["x"][0],
        "gains1": np.concatenate([a["norm_mix"], a["norm_mlp"]]),
        "gains2": np.concatenate([a["norm_final"][None], a["norm1_g_2"], a["norm2_g_2"],
                                  np.concatenate([a["out_norm_a_2"], a["out_norm_b_2"]], 1)]),
        "conv_w": a["conv_w"].reshape(LAYERS, TAPS, KW, P).transpose(3, 0, 2, 1).reshape(
            P, LAYERS, KW * TAPS),
        "b_ada": a["b_ada_2"][0].reshape(6, D),
        "c_cols": a["c_2"][0].reshape(KD, P).T,
        "kept_in": kept_table(),
        "rope_in": rope_table(),
        "na_mask_in": na_column_mask(),
        "t5_in": t5,
        "t5_hot": t5_table_of_distance(),
        "rpb_pad": rpb[:, NA_ROWS - ROWS:NA_ROWS - ROWS + NA_DR].reshape(1, -1),
        "sinks": a["sink_a_2"][0],
        "sub_keys": a["sub_keys_2"][0].transpose(3, 0, 1, 2).reshape(P, N_QUERY, PK),
        "gain_out": a["final_g_2"].reshape(1, D),
    }
    arrays = {k: np.ascontiguousarray(v) for k, v in arrays.items()}
    nc = bacc.Bacc("TRN2", target_bir_lowering=False, num_devices=1)
    args = {k: nc.dram_tensor(k, v.shape, F32, kind="ExternalInput").ap() for k, v in arrays.items()}
    out = nc.dram_tensor("out", (T, D), F32, kind="ExternalOutput").ap()
    build(nc, out=out, **args)
    r = run_bass_kernel_spmd(nc, [arrays], core_ids=[0])
    return r.results[0]["out"].reshape(1, T, D)
```
